# Optimizing a Trainium2 kernel written in Bass

```python
import jax
import jax.numpy as jnp
from jax import lax
import numpy as np

D_MODEL = 1024
BATCH = 1
SEQ = 1024
DEPTH = 2

GRID_W = 64
CTX_LEN = 256
HEAD_DIM = 64
A_HEADS = 8
A_KV_HEADS = 2
WINDOW = 128
A_BLOCK = 128
A_WIDTH = A_HEADS * HEAD_DIM
A_KV_WIDTH = A_KV_HEADS * HEAD_DIM
A_IN = A_WIDTH + 2 * A_KV_WIDTH
B_GROUPS = 8
B_WIDTH = 512
B_GROUP_DIM = B_WIDTH // B_GROUPS
CHUNK = 128
AB_IN = A_IN + 2 * B_WIDTH
AB_OUT = A_WIDTH + B_WIDTH
C_HEADS = 16
C_WIDTH = C_HEADS * HEAD_DIM
NA_ROWS = 8
NA_COLS = 16
NA_COL_BLOCK = 16
NA_KEY_COLS = 32
RPB_R = 2 * NA_ROWS - 1
RPB_C = 2 * NA_COLS - 1
D_FF = 4 * D_MODEL
ROPE_BASE = 10000.0
LN_EPS = 1e-5
NEG_INF = -1e30
DEEPNORM_ALPHA = (2 * DEPTH) ** 0.25
DEEPNORM_BETA = (8 * DEPTH) ** -0.25
N_EVEN = (DEPTH + 1) // 2
N_ODD = DEPTH // 2

kernel_name = 'hybrid_window_gmlp_natten_prefix_dit'

def _layer_norm(x, g, b):
    xf = x.astype(jnp.float32)
    mu = jnp.mean(xf, axis=-1, keepdims=True)
    var = jnp.mean(jnp.square(xf - mu), axis=-1, keepdims=True)
    y = (xf - mu) * lax.rsqrt(var + LN_EPS)
    return (y * g.astype(jnp.float32) + b.astype(jnp.float32)).astype(x.dtype)

def _modulation(cond, w, b):
    return jnp.split(jax.nn.silu(cond) @ w + b, 6, axis=-1)

def _axial_rope(n_tok):
    t = jnp.arange(n_tok)
    row = (t // GRID_W).astype(jnp.float32)
    col = (t % GRID_W).astype(jnp.float32)
    n_pairs = HEAD_DIM // 4
    freqs = ROPE_BASE ** (-jnp.arange(n_pairs, dtype=jnp.float32) / n_pairs)
    ang = jnp.concatenate([row[:, None] * freqs, col[:, None] * freqs], axis=-1)
    return jnp.cos(ang), jnp.sin(ang)

def _apply_rope(x, cos, sin):
    xf = x.astype(jnp.float32)
    x1, x2 = xf[..., 0::2], xf[..., 1::2]
    cc, ss = cos[:, None, :], sin[:, None, :]
    out = jnp.stack([x1 * cc - x2 * ss, x1 * ss + x2 * cc], axis=-1).reshape(x.shape)
    return out.astype(x.dtype)

def _joint_softmax(s_loc, s_ctx, s_sink=None):
    m = jnp.maximum(jnp.max(s_loc, axis=-1, keepdims=True), jnp.max(s_ctx, axis=-1, keepdims=True))
    if s_sink is not None:
        m = jnp.maximum(m, s_sink)
    e_loc = jnp.exp(s_loc - m)
    e_ctx = jnp.exp(s_ctx - m)
    denom = jnp.sum(e_loc, axis=-1, keepdims=True) + jnp.sum(e_ctx, axis=-1, keepdims=True)
    if s_sink is not None:
        denom = denom + jnp.exp(s_sink - m)
    return e_loc / denom, e_ctx / denom

def _context_attention(qc, kc, vc, sink):
    B, L, H, D = qc.shape
    hkv = kc.shape[2]
    g = H // hkv
    qg = qc.reshape(B, L, hkv, g, D)
    s = jnp.einsum('bqhgd,bkhd->bhgqk', qg, kc).astype(jnp.float32) * (D ** -0.5)
    if sink is not None:
        s_sink = jnp.broadcast_to(sink.astype(jnp.float32).reshape(hkv, g)[None, :, :, None, None], (B, hkv, g, L, 1))
        s = jnp.concatenate([s, s_sink], axis=-1)
    p = jax.nn.softmax(s, axis=-1)[..., :L].astype(vc.dtype)
    o = jnp.einsum('bhgqk,bkhd->bqhgd', p, vc)
    return o.reshape(B, L, H * D)

def _window_attention(q, k, v, kc, vc, sink):
    B, S, H, D = q.shape
    hkv = k.shape[2]
    g = H // hkv
    nb = S // A_BLOCK
    nk = 3 * A_BLOCK
    scale = D ** -0.5
    qb = q.reshape(B, nb, A_BLOCK, hkv, g, D)
    pad = ((0, 0), (A_BLOCK, A_BLOCK), (0, 0), (0, 0))
    kp = jnp.pad(k, pad).reshape(B, nb + 2, A_BLOCK, hkv, D)
    vp = jnp.pad(v, pad).reshape(B, nb + 2, A_BLOCK, hkv, D)
    kw = jnp.concatenate([kp[:, :-2], kp[:, 1:-1], kp[:, 2:]], axis=2)
    vw = jnp.concatenate([vp[:, :-2], vp[:, 1:-1], vp[:, 2:]], axis=2)
    qpos = np.arange(nb)[:, None, None] * A_BLOCK + np.arange(A_BLOCK)[None, :, None]
    kpos = np.arange(nb)[:, None, None] * A_BLOCK - A_BLOCK + np.arange(nk)[None, None, :]
    band = (np.abs(qpos - kpos) <= WINDOW) & (kpos >= 0) & (kpos < S)
    s_loc = jnp.einsum('bnqhgd,bnkhd->bhgnqk', qb, kw).astype(jnp.float32) * scale
    s_loc = jnp.where(band, s_loc, NEG_INF)
    s_ctx = jnp.einsum('bnqhgd,bkhd->bhgnqk', qb, kc).astype(jnp.float32) * scale
    s_sink = sink.astype(jnp.float32).reshape(hkv, g)[None, :, :, None, None, None]
    p_loc, p_ctx = _joint_softmax(s_loc, s_ctx, s_sink)
    o = (jnp.einsum('bhgnqk,bnkhd->bnqhgd', p_loc.astype(v.dtype), vw)
         + jnp.einsum('bhgnqk,bkhd->bnqhgd', p_ctx.astype(v.dtype), vc))
    return o.reshape(B, S, H * D)

def _spatial_gating(u, gv, ln_g, ln_b, w_s, b_s):
    B, S, _ = u.shape
    nc = S // CHUNK
    vn = _layer_norm(gv, ln_g, ln_b).reshape(B, nc, CHUNK, B_GROUPS, B_GROUP_DIM)
    mixed = jnp.einsum('gpq,bnqgc->bnpgc', w_s, vn) + b_s.T[None, None, :, :, None]
    return u * mixed.reshape(B, S, B_WIDTH)

def _mixer_ab(h, hc, w_in, w_out, sink, ln_g, ln_b, w_s, b_s, cos, sin, need_ctx_out):
    B, S, _ = h.shape
    L = hc.shape[1]
    z = h @ w_in
    q = _apply_rope(z[..., :A_WIDTH].reshape(B, S, A_HEADS, HEAD_DIM), cos, sin)
    k = _apply_rope(z[..., A_WIDTH:A_WIDTH + A_KV_WIDTH].reshape(B, S, A_KV_HEADS, HEAD_DIM), cos, sin)
    v = z[..., A_WIDTH + A_KV_WIDTH:A_IN].reshape(B, S, A_KV_HEADS, HEAD_DIM)
    u = jax.nn.gelu(z[..., A_IN:A_IN + B_WIDTH], approximate=False)
    gv = jax.nn.gelu(z[..., A_IN + B_WIDTH:], approximate=False)
    zkv = hc @ w_in[:, A_WIDTH:A_IN]
    kc = zkv[..., :A_KV_WIDTH].reshape(B, L, A_KV_HEADS, HEAD_DIM)
    vc = zkv[..., A_KV_WIDTH:].reshape(B, L, A_KV_HEADS, HEAD_DIM)
    a_out = _window_attention(q, k, v, kc, vc, sink)
    b_out = _spatial_gating(u, gv, ln_g, ln_b, w_s, b_s)
    y = jnp.concatenate([a_out, b_out], axis=-1) @ w_out
    yc = None
    if need_ctx_out:
        qc = (hc @ w_in[:, :A_WIDTH]).reshape(B, L, A_HEADS, HEAD_DIM)
        zc = hc @ w_in[:, A_IN:]
        uc = jax.nn.gelu(zc[..., :B_WIDTH], approximate=False)
        gvc = jax.nn.gelu(zc[..., B_WIDTH:], approximate=False)
        ac_out = _context_attention(qc, kc, vc, sink)
        bc_out = _spatial_gating(uc, gvc, ln_g, ln_b, w_s, b_s)
        yc = jnp.concatenate([ac_out, bc_out], axis=-1) @ w_out
    return y, yc

def _neighbourhood_attention(q, k, v, kc, vc, rpb):
    B, S, H, D = q.shape
    rows = S // GRID_W
    kh = min(NA_ROWS, rows)
    n_cb = GRID_W // NA_COL_BLOCK
    scale = D ** -0.5
    qcol = np.arange(GRID_W).reshape(n_cb, NA_COL_BLOCK)
    q_start = np.clip(qcol - NA_COLS // 2, 0, GRID_W - NA_COLS)
    k_start = np.clip(np.arange(n_cb) * NA_COL_BLOCK - NA_COLS // 2, 0, GRID_W - NA_KEY_COLS)
    key_cols = k_start[:, None] + np.arange(NA_KEY_COLS)[None, :]
    kcb = key_cols[:, None, :]
    col_ok = (kcb >= q_start[..., None]) & (kcb < q_start[..., None] + NA_COLS)
    mask = np.broadcast_to(col_ok[:, :, None, :], (n_cb, NA_COL_BLOCK, kh, NA_KEY_COLS)).reshape(n_cb, NA_COL_BLOCK, kh * NA_KEY_COLS)
    dc_idx = np.clip(kcb - qcol[..., None] + NA_COLS - 1, 0, RPB_C - 1)
    qg = q.reshape(B, rows, n_cb, NA_COL_BLOCK, H, D)
    kg = k.reshape(B, rows, GRID_W, H, D)
    vg = v.reshape(B, rows, GRID_W, H, D)

    def row_block(r):
        r0 = jnp.clip(r - kh // 2, 0, rows - kh)
        k_rows = lax.dynamic_slice_in_dim(kg, r0, kh, axis=1)
        v_rows = lax.dynamic_slice_in_dim(vg, r0, kh, axis=1)
        kb = k_rows[:, :, key_cols].transpose(0, 2, 1, 3, 4, 5).reshape(B, n_cb, kh * NA_KEY_COLS, H, D)
        vb = v_rows[:, :, key_cols].transpose(0, 2, 1, 3, 4, 5).reshape(B, n_cb, kh * NA_KEY_COLS, H, D)
        qr = lax.dynamic_index_in_dim(qg, r, axis=1, keepdims=False)
        dr = r0 + jnp.arange(kh) - r + NA_ROWS - 1
        bias = jnp.take(rpb, dr, axis=1)[:, :, dc_idx]
        bias = bias.transpose(0, 2, 3, 1, 4).reshape(H, n_cb, NA_COL_BLOCK, kh * NA_KEY_COLS).astype(jnp.float32)
        s_loc = jnp.einsum('bjqhd,bjkhd->bhjqk', qr, kb).astype(jnp.float32) * scale + bias
        s_loc = jnp.where(mask, s_loc, NEG_INF)
        s_ctx = jnp.einsum('bjqhd,bkhd->bhjqk', qr, kc).astype(jnp.float32) * scale
        p_loc, p_ctx = _joint_softmax(s_loc, s_ctx)
        o = (jnp.einsum('bhjqk,bjkhd->bjqhd', p_loc.astype(v.dtype), vb)
             + jnp.einsum('bhjqk,bkhd->bjqhd', p_ctx.astype(v.dtype), vc))
        return o.reshape(B, GRID_W, H * D)

    out = lax.map(row_block, jnp.arange(rows))
    return out.transpose(1, 0, 2, 3).reshape(B, S, H * D)

def _mixer_c(h, hc, w_in, w_out, rpb, need_ctx_out):
    B, S, _ = h.shape
    L = hc.shape[1]
    z = h @ w_in
    q = z[..., :C_WIDTH].reshape(B, S, C_HEADS, HEAD_DIM)
    k = z[..., C_WIDTH:2 * C_WIDTH].reshape(B, S, C_HEADS, HEAD_DIM)
    v = z[..., 2 * C_WIDTH:].reshape(B, S, C_HEADS, HEAD_DIM)
    zkv = hc @ w_in[:, C_WIDTH:]
    kc = zkv[..., :C_WIDTH].reshape(B, L, C_HEADS, HEAD_DIM)
    vc = zkv[..., C_WIDTH:].reshape(B, L, C_HEADS, HEAD_DIM)
    y = _neighbourhood_attention(q, k, v, kc, vc, rpb) @ w_out
    yc = None
    if need_ctx_out:
        qc = (hc @ w_in[:, :C_WIDTH]).reshape(B, L, C_HEADS, HEAD_DIM)
        yc = _context_attention(qc, kc, vc, None) @ w_out
    return y, yc

def _squared_relu_mlp(h, w1, w2):
    return jnp.square(jax.nn.relu(h @ w1)) @ w2

def setup_inputs(seed: int = 0) -> dict:
    key = jax.random.key(seed)
    ks = jax.random.split(key, 24)
    f32 = jnp.float32

    def nrm(k, shape, scale):
        return jax.random.normal(k, shape, f32) * scale

    return {
        'x': nrm(ks[0], (BATCH, SEQ, D_MODEL), 1.0),
        'c': nrm(ks[1], (BATCH, D_MODEL), 1.0),
        'ctx': nrm(ks[2], (BATCH, CTX_LEN, D_MODEL), 1.0),
        'c_ctx': nrm(ks[3], (D_MODEL,), 1.0),
        'w_mod': nrm(ks[4], (DEPTH, D_MODEL, 6 * D_MODEL), 0.5 * D_MODEL ** -0.5),
        'b_mod': nrm(ks[5], (DEPTH, 6 * D_MODEL), 0.02),
        'ab_w_in': nrm(ks[6], (N_EVEN, D_MODEL, AB_IN), D_MODEL ** -0.5),
        'a_sink': nrm(ks[7], (N_EVEN, A_HEADS), 1.0),
        'b_ln_g': 1.0 + nrm(ks[8], (N_EVEN, B_WIDTH), 0.02),
        'b_ln_b': nrm(ks[9], (N_EVEN, B_WIDTH), 0.02),
        'b_ws': nrm(ks[10], (N_EVEN, B_GROUPS, CHUNK, CHUNK), CHUNK ** -0.5),
        'b_bs': 1.0 + nrm(ks[11], (N_EVEN, B_GROUPS, CHUNK), 0.02),
        'ab_w_out': nrm(ks[12], (N_EVEN, AB_OUT, D_MODEL), DEEPNORM_BETA * AB_OUT ** -0.5),
        'c_w_in': nrm(ks[13], (N_ODD, D_MODEL, 3 * C_WIDTH), D_MODEL ** -0.5),
        'c_rpb': nrm(ks[14], (N_ODD, C_HEADS, RPB_R, RPB_C), 0.1),
        'c_w_out': nrm(ks[15], (N_ODD, C_WIDTH, D_MODEL), DEEPNORM_BETA * C_WIDTH ** -0.5),
        'ln1_g': 1.0 + nrm(ks[16], (DEPTH, D_MODEL), 0.02),
        'ln1_b': nrm(ks[17], (DEPTH, D_MODEL), 0.02),
        'mlp_w1': nrm(ks[18], (DEPTH, D_MODEL, D_FF), D_MODEL ** -0.5),
        'mlp_w2': nrm(ks[19], (DEPTH, D_FF, D_MODEL), DEEPNORM_BETA * D_FF ** -0.5),
        'ln2_g': 1.0 + nrm(ks[20], (DEPTH, D_MODEL), 0.02),
        'ln2_b': nrm(ks[21], (DEPTH, D_MODEL), 0.02),
    }

def reference(x, c, ctx, c_ctx, w_mod, b_mod, ab_w_in, a_sink, b_ln_g, b_ln_b, b_ws, b_bs, ab_w_out,
              c_w_in, c_rpb, c_w_out, ln1_g, ln1_b, mlp_w1, mlp_w2, ln2_g, ln2_b):
    S = x.shape[1]
    cos, sin = _axial_rope(S)
    for l in range(DEPTH):
        last = l == DEPTH - 1
        i = l // 2
        sh_a, sc_a, g_a, sh_m, sc_m, g_m = [m[:, None, :] for m in _modulation(c, w_mod[l], b_mod[l])]
        csh_a, csc_a, cg_a, csh_m, csc_m, cg_m = _modulation(c_ctx, w_mod[l], b_mod[l])
        h = x * (1 + sc_a) + sh_a
        hc = ctx * (1 + csc_a) + csh_a
        if l % 2 == 0:
            y, yc = _mixer_ab(h, hc, ab_w_in[i], ab_w_out[i], a_sink[i], b_ln_g[i], b_ln_b[i],
                              b_ws[i], b_bs[i], cos, sin, not last)
        else:
            y, yc = _mixer_c(h, hc, c_w_in[i], c_w_out[i], c_rpb[i], not last)
        x = _layer_norm(DEEPNORM_ALPHA * x + g_a * y, ln1_g[l], ln1_b[l])
        x = _layer_norm(DEEPNORM_ALPHA * x + g_m * _squared_relu_mlp(x * (1 + sc_m) + sh_m, mlp_w1[l], mlp_w2[l]),
                        ln2_g[l], ln2_b[l])
        if not last:
            ctx = _layer_norm(DEEPNORM_ALPHA * ctx + cg_a * yc, ln1_g[l], ln1_b[l])
            ctx = _layer_norm(DEEPNORM_ALPHA * ctx + cg_m * _squared_relu_mlp(ctx * (1 + csc_m) + csh_m, mlp_w1[l], mlp_w2[l]),
                              ln2_g[l], ln2_b[l])
    return x


_drawn_inputs = setup_inputs


def setup_inputs(seed=0):
    import zlib

    import numpy as np

    out = dict(_drawn_inputs(seed))
    spreads = {}
    factors = {'ctx': 5.439,
     'b_mod': 3.33,
     'a_sink': 64.0,
     'b_ln_g': 61.98,
     'b_ln_b': 61.028,
     'b_bs': 62.104,
     'c_rpb': 64.0}
    for name, (base, spread) in spreads.items():
        noise = np.random.default_rng([zlib.crc32(name.encode()), seed]).standard_normal(out[name].shape)
        drawn = base * np.exp(spread * noise) if base else spread * noise
        out[name] = jnp.asarray(drawn.astype(out[name].dtype))
    for name, factor in factors.items():
        out[name] = (out[name] * factor).astype(out[name].dtype)
    return out
```

```python
import numpy as np
import concourse.bass as bass
from concourse import mybir

F32 = mybir.dt.float32
F32R = mybir.dt.float32r
ALU = mybir.AluOpType
ACT = mybir.ActivationFunctionType
AXX = mybir.AxisListType.X

P = 128
D = 1024
KT = D // P
SEQ, CTX = 1024, 256
TOK = SEQ + CTX
XT, CT = SEQ // P, CTX // P
DEPTH = 2
HD = 64
FF = 4 * D
FC = 256
NCH = FF // FC
ALPHA = (2 * DEPTH) ** 0.25
EPS = 1e-5
NEG = -1e30
GRID_W, NA_ROWS, NA_COLS = 64, 8, 16
RPB_R, RPB_C = 2 * NA_ROWS - 1, 2 * NA_COLS - 1
RP_ROWS, RP_W = RPB_R + 2, 128
SH_A, SC_A, G_A, SH_M, SC_M, G_M = range(6)

BASE = 20608
END = 229368


def wait(eng, sem, value):
    if isinstance(value, int) and value <= 0:
        return
    eng.wait_ge(sem, value)


def address(eng, value):
    return value if isinstance(value, int) else eng.snap(value)


class Place:

    def __init__(self, nc, tag, at=BASE):
        self.nc, self.tag, self.at = nc, tag, at

    def __call__(self, name, shape, dt=F32):
        size = int(np.prod(shape[1:])) * 4
        t = self.nc.alloc_sbuf_tensor_at(f"{self.tag}_{name}", shape, dt, offset=self.at)
        self.at += (size + 31) // 32 * 32
        assert self.at <= END, (self.tag, name, self.at)
        return t


class Kept:

    def __init__(self, nc):
        self.nc, self.live, self.dead = nc, [], []

    def sem(self, name):
        s = self.nc.alloc_semaphore(name)
        self.live.append(s)
        return s

    def clear_last(self, dve):
        for s in self.dead:
            dve.sem_clear(s)

    def end_stage(self):
        for s in self.dead:
            self.nc.release_semaphore(s)
        self.dead, self.live = self.live, []


def f32(ap):
    return ap.bitcast(F32)


def groups_of(tokens):
    return [(a, min(512, tokens - a)) for a in range(0, tokens, 512)]


def stage_modulation(nc, io, k):
    sb = Place(nc, "mod")
    NB = 6 * D // 512
    RING = 4
    wbuf = sb("w", [P, RING, KT, 512])
    crow = sb("crow", [2 * KT, P])
    csil = sb("csil", [2 * KT, P])
    ccol = sb("ccol", [P, 2 * KT])
    brow = sb("brow", [48, 2, P])
    bcol = sb("bcol", [P, 2, 48])
    grow = sb("grow", [2 * KT, 4, P])
    zero = sb("zero", [P, RP_ROWS, P])
    s_in, s_pad, s_padz = k.sem("mod_in"), k.sem("mod_pad"), k.sem("mod_zero")
    s_silu, s_tr, s_col = k.sem("mod_silu"), k.sem("mod_tr"), k.sem("mod_col")
    s_const = k.sem("const")
    s_w = [k.sem(f"mod_w{i}") for i in range(RING)]
    s_mm, s_add, s_gt, s_gr, s_out = [k.sem(f"mod_{x}") for x in ("mm", "add", "gt", "gr", "out")]
    ps, pt = k.bank[0], k.bank[1]
    N = 2 * NB
    with nc.Block() as block:
        @block.sync
        def _(sp):
            for name, t in (("ident", k.ident), ("sel", k.sel), ("eps", k.eps)):
                sp.dma_start(t[:, :], io[name]).then_inc(s_const, 16)
            sp.dma_start(crow[0:KT, :], io["c"].rearrange("a (k p) -> (a k) p", p=P)).then_inc(s_in, 16)
            sp.dma_start(crow[KT:2 * KT, :], io["c_ctx"].rearrange("(k p) -> k p", p=P)).then_inc(s_in, 16)
            sp.dma_start(brow[:, :, :], io["b_mod"].rearrange("l (j p) -> j l p", p=P)).then_inc(s_in, 16)
            for n in range(N):
                if n >= RING:
                    sp.wait_ge(s_mm, n - RING + 1)
                src = io["w_mod"][n // NB].rearrange("(k p) n -> p k n", p=P)[:, :, (n % NB) * 512:(n % NB + 1) * 512]
                sp.dma_start(wbuf[:, n % RING, :, :], src).then_inc(s_w[n % RING], 16)
            for g in range(4):
                sp.wait_ge(s_gr, g + 1)
                sp.dma_start(k.gate_dram[g // 2, g % 2], grow[:, g, :]).then_inc(s_out, 16)
            sp.wait_ge(s_out, 64)
            sp.wait_ge(s_padz, 1)
            sp.dma_start(k.rp_dram.rearrange("h r x -> h (r x)"), zero[0:16, :, :].rearrange("h r x -> h (r x)")).then_inc(s_pad, 16)
            sp.wait_ge(s_pad, 16)
            sp.dma_start(k.rp_dram[:, 1:1 + RPB_R, 48:48 + RPB_C], io["c_rpb"][0]).then_inc(s_pad, 16)
            sp.wait_ge(s_pad, 32)
            sp.wait_ge(s_const, 48)

        @block.gpsimd
        def _(pool):
            pool.memset(zero[:, :, :], 0.0).then_inc(s_padz, 1)

        @block.scalar
        def _(act):
            act.wait_ge(s_in, 48)
            act.activation(csil[:, :], crow[:, :], ACT.Silu).then_inc(s_silu, 1)

        @block.tensor
        def _(pe):
            pe.wait_ge(s_silu, 1)
            pe.wait_ge(s_const, 48)
            pe.transpose(pt[:, 0:2 * KT], csil[:, :], k.ident[0:2 * KT, 0:2 * KT]).then_inc(s_tr, 1)
            for l in range(2):
                pe.transpose(pt[:, 64 + 64 * l:64 + 64 * l + 48], brow[:, l, :], k.ident[0:48, 0:48]).then_inc(s_tr, 1)
            pe.wait_ge(s_col, 2)
            for n in range(N):
                pe.wait_ge(s_w[n % RING], 16 * (n // RING + 1))
                if n >= 1:
                    pe.wait_ge(s_add, n)
                for j in range(4):
                    for kt in range(KT):
                        mm = pe.matmul(ps[:, 2 * j:2 * j + 2], wbuf[:, n % RING, kt, j * P:(j + 1) * P],
                                       ccol[:, kt:2 * KT:KT], start=kt == 0, stop=kt == KT - 1)
                mm.then_inc(s_mm, 1)
            pe.wait_ge(s_add, N + 4)
            for g in range(4):
                part = G_A if g % 2 == 0 else G_M
                if g >= 1:
                    pe.wait_ge(s_gr, g)
                pe.transpose(pt[0:2 * KT, 0:P], k.mod[:, g // 2, part * KT:(part + 1) * KT, :].rearrange("p j c -> p (j c)"),
                             k.ident[:, :]).then_inc(s_gt, 1)

        @block.vector
        def _(dve):
            k.clear_last(dve)
            dve.wait_ge(s_tr, 3)
            dve.tensor_copy(ccol[:, :], pt[:, 0:2 * KT]).then_inc(s_col, 1)
            dve.tensor_copy(bcol[:, :, :], pt[:, 64:192].rearrange("p (l j) -> p l j", l=2)[:, :, 0:48]).then_inc(s_col, 1)
            dve.wait_ge(s_col, 2)
            for n in range(N):
                l, j = n // NB, 4 * (n % NB)
                dve.wait_ge(s_mm, n + 1)
                dve.tensor_tensor(k.mod[:, l, j:j + 4, :], ps[:, 0:8].rearrange("p (j c) -> p j c", c=2),
                                  bcol[:, l, j:j + 4].unsqueeze(2).broadcast_to([P, 4, 2]), ALU.add).then_inc(s_add, 1)
            dve.wait_ge(s_add, N)
            for l in range(2):
                for part in (SC_A, SC_M):
                    at = k.mod[:, l, part * KT:(part + 1) * KT, :]
                    dve.tensor_scalar(at, at, 1.0, None, ALU.add).then_inc(s_add, 1)
            for g in range(4):
                dve.wait_ge(s_gt, g + 1)
                dve.tensor_copy(grow[:, g, :], pt[0:2 * KT, 0:P]).then_inc(s_gr, 1)


def stage_rows(nc, io, k, layer, kind):
    tag = f"r{layer}{kind}"
    sb = Place(nc, tag, k.after_ht)
    tiles = XT if (layer == DEPTH - 1 and kind) else XT + CT
    last = layer == DEPTH - 1 and kind == 2
    sem = lambda n: k.sem(f"{tag}_{n}")
    if kind == 2:
        y = k.y
        sb.at = k.after_y
    if kind == 1:
        wh, wl = sb("wh", [P, KT, D], F32R), sb("wl", [P, KT, D], F32R)
        raw = sb("raw", [P, 2, D])
        cath, catl = sb("cath", [P, 2, KT, P], F32R), sb("catl", [P, 2, KT, P], F32R)
    nbuf = 1 if kind == 1 else 2
    xin = sb("xin", [P, nbuf, D])
    res = sb("res", [P, nbuf, D])
    modt = sb("modt", [P, KT, P])
    if kind:
        gate = sb("gate", [P, 2, D])
        lng, lnb = sb("lng", [P, D]), sb("lnb", [P, D])
        stats, mv = sb("stats", [P, 2, 2, 6]), sb("mv", [P, 2, 2])
        rstd = sb("rstd", [P, 2, 2])
    s_row, s_x = sem("rows"), [sem(f"x{i}") for i in range(nbuf)]
    s_raw = [sem(f"raw{i}") for i in range(2)]
    s_high, s_low, s_yps = sem("high"), sem("low"), sem("yps")
    s_dve, s_std, s_g, s_b, s_tr, s_mod, s_hh, s_hl = [sem(x) for x in ("dve", "std", "g", "b", "tr", "mod", "hh", "hl")]
    s_store = [sem(f"store{i}") for i in range(nbuf)]
    NW = KT if kind == 1 else 0
    next_layer, msh, msc = (layer, SH_M, SC_M) if kind == 1 else ((layer, SH_A, SC_A) if kind == 0 else (layer + 1, SH_A, SC_A))
    ln = 1 if kind == 1 else 2
    cond = lambda t: 0 if t < XT else 1
    src = lambda t: (io["x"][0] if t < XT else io["ctx"][0])[(t % XT) * P:(t % XT + 1) * P, :] if (layer == 0 and kind < 2) \
        else k.x_dram[t * P:(t + 1) * P, :]
    done = (lambda t: (s_b, t + 1)) if kind else (lambda t: (s_x[t % nbuf], 16 * (t // nbuf + 1)))
    final = lambda t: (res if kind else xin)[:, t % nbuf, :]
    C = 6

    with nc.Block() as block:
        @block.sync
        def _(sp):
            if kind:
                sp.dma_start(lng[:, :], bass.AP(tensor=io[f"ln{ln}_g"].tensor, offset=layer * D, ap=[[0, P], [1, D]])).then_inc(s_row, 16)
                sp.dma_start(lnb[:, :], bass.AP(tensor=io[f"ln{ln}_b"].tensor, offset=layer * D, ap=[[0, P], [1, D]])).then_inc(s_row, 16)
                for c in range(2):
                    at = ((layer * 2 + kind - 1) * 2 * KT + c) * P
                    sp.dma_start(gate[:, c, :].rearrange("p (j q) -> p j q", q=P),
                                 bass.AP(tensor=k.gate_dram.tensor, offset=at, ap=[[0, P], [2 * P, KT], [1, P]])).then_inc(s_row, 16)
            w_out = io["ab_w_out" if layer == 0 else "c_w_out"][0]
            def slice_in(u):
                if u >= NW + tiles:
                    return
                if u >= 2:
                    sp.wait_ge(s_low, u - 1)
                if u < NW:
                    sp.dma_start(raw[:, u % 2, :], w_out[u * P:(u + 1) * P, :]).then_inc(s_raw[u % 2], 16)
                else:
                    t = u - NW
                    sp.dma_start(raw[:, u % 2, :].rearrange("p (j q) -> p j q", q=P),
                                 k.cat_dram.rearrange("(j p) t -> p j t", p=P)[:, :, t * P:(t + 1) * P]).then_inc(s_raw[u % 2], 16)

            def residual_in(t):
                if t >= tiles:
                    return
                if t >= nbuf:
                    if kind:
                        sp.wait_ge(s_dve, C * (t - nbuf) + 2)
                    else:
                        sp.wait_ge(s_tr, t - nbuf + 1)
                sp.dma_start(xin[:, t % nbuf, :], src(t)).then_inc(s_x[t % nbuf], 16)

            for t in range(nbuf):
                residual_in(t)
            if kind == 1:
                for u in range(NW + 2):
                    slice_in(u)
            for t in range(tiles):
                if kind == 1:
                    slice_in(NW + 2 + t)
                residual_in(t + nbuf)
                if kind:
                    sp.wait_ge(s_b, t + 1)
                    dst = k.out[0, t * P:(t + 1) * P, :] if last else k.x_dram[t * P:(t + 1) * P, :]
                    sp.dma_start(dst, res[:, t % nbuf, :]).then_inc(s_store[t % nbuf], 16)
            if kind:
                for i in range(nbuf):
                    sp.wait_ge(s_store[i], 16 * (tiles // nbuf))

        @block.gpsimd
        def _(pool):
            if kind:
                pool.wait_ge(s_row, 64)
            for t in range(tiles):
                if kind:
                    r = res[:, t % nbuf, :]
                    pool.wait_ge(s_dve, C * t + 6)
                    pool.tensor_tensor(r, r, lng[:, :], ALU.mult).then_inc(s_g, 1)
                    pool.wait_ge(s_g, t + 1)
                    pool.tensor_tensor(r, r, lnb[:, :], ALU.add).then_inc(s_b, 1)

        @block.scalar
        def _(act):
            def high(u):
                act.wait_ge(s_raw[u % 2], 16 * (u // 2 + 1))
                if u < NW:
                    out = wh[:, u, :]
                else:
                    t = u - NW
                    if t >= 2:
                        act.wait_ge(s_yps, t - 1)
                    out = cath[:, t % 2, :, :].rearrange("p j q -> p (j q)")
                act.activation(out, raw[:, u % 2, :], ACT.Copy).then_inc(s_high, 1)

            for u in range(NW):
                high(u)
            if kind == 1:
                high(NW)
            for t in range(tiles):
                if kind == 1 and t + 1 < tiles:
                    high(NW + t + 1)
                if kind:
                    act.wait_ge(s_dve, C * t + 4)
                    act.activation(rstd[:, t % 2, 0:1], mv[:, t % 2, 1:2], ACT.Sqrt, bias=k.eps[:, 0:1]).then_inc(s_std, 1)
                if not last:
                    act.wait_ge(s_tr, t + 1)
                    if t >= 1:
                        act.wait_ge(s_hl, t)
                    for j in range(KT):
                        col = lambda part: k.mod[:, next_layer, part * KT + j, cond(t):cond(t) + 1]
                        a = act.activation(modt[:, j, :], k.bank[4 + 2 * (t % 2) + j // 4][:, (j % 4) * P:(j % 4 + 1) * P], ACT.Identity,
                                           scale=col(msc), bias=col(msh))
                    a.then_inc(s_mod, 1)
                    act.wait_ge(s_mod, t + 1)
                    act.activation(k.hth[:, :, t * P:(t + 1) * P], modt[:, :, :], ACT.Copy).then_inc(s_hh, 1)

        @block.vector
        def _(dve):
            k.clear_last(dve)
            def low(u):
                dve.wait_ge(s_high, u + 1)
                if u < NW:
                    h, out = wh[:, u, :], wl[:, u, :]
                else:
                    t = u - NW
                    h = cath[:, t % 2, :, :].rearrange("p j q -> p (j q)")
                    out = catl[:, t % 2, :, :].rearrange("p j q -> p (j q)")
                dve.tensor_tensor(out, raw[:, u % 2, :], f32(h), ALU.subtract).then_inc(s_low, 1)

            def split_ht(t):
                dve.wait_ge(s_hh, t + 1)
                dve.tensor_tensor(k.htl[:, :, t * P:(t + 1) * P], modt[:, :, :], f32(k.hth[:, :, t * P:(t + 1) * P]),
                                  ALU.subtract).then_inc(s_hl, 1)

            for u in range(NW):
                low(u)
            if kind == 1:
                low(NW)
            if kind:
                dve.wait_ge(s_row, 64)
            for t in range(tiles):
                if kind == 1 and t + 1 < tiles:
                    low(NW + t + 1)
                if kind:
                    n, r = C * t, res[:, t % nbuf, :]
                    if t >= nbuf:
                        dve.wait_ge(s_store[t % nbuf], 16 * (t // nbuf))
                        if not last:
                            dve.wait_ge(s_tr, t - nbuf + 1)
                    g = gate[:, cond(t), :]
                    if kind == 1:
                        dve.wait_ge(s_yps, t + 1)
                        b = 2 * (t % 2)
                        for half in range(2):
                            i = dve.tensor_tensor(r[:, half * 512:half * 512 + 512], k.bank[b + half][:, :],
                                                  g[:, half * 512:half * 512 + 512], ALU.mult)
                        i.then_inc(s_dve, 1)
                    else:
                        dve.tensor_tensor(r, y[:, t, :], g, ALU.mult).then_inc(s_dve, 1)
                    dve.wait_ge(s_dve, n + 1)
                    dve.wait_ge(s_x[t % nbuf], 16 * (t // nbuf + 1))
                    dve.scalar_tensor_tensor(out=r, in0=xin[:, t % nbuf, :], scalar=ALPHA, in1=r, op0=ALU.mult,
                                             op1=ALU.add).then_inc(s_dve, 1)
                    dve.wait_ge(s_dve, n + 2)
                    for half in range(2):
                        i = dve.bn_stats(stats[:, t % 2, half, :], r[:, half * 512:half * 512 + 512])
                    i.then_inc(s_dve, 1)
                    dve.wait_ge(s_dve, n + 3)
                    dve.bn_aggr(mv[:, t % 2, :], stats[:, t % 2, :, :].rearrange("p a b -> p (a b)")).then_inc(s_dve, 1)
                    if t >= 1 and not last:
                        split_ht(t - 1)
                    dve.wait_ge(s_std, t + 1)
                    dve.reciprocal(rstd[:, t % 2, 1:2], rstd[:, t % 2, 0:1]).then_inc(s_dve, 1)
                    dve.wait_ge(s_dve, n + 5)
                    dve.tensor_scalar(r, r, mv[:, t % 2, 0:1], rstd[:, t % 2, 1:2], ALU.subtract, ALU.mult).then_inc(s_dve, 1)
                elif t >= 1:
                    split_ht(t - 1)
            if not last:
                split_ht(tiles - 1)

        @block.tensor
        def _(pe):
            def transposes(t):
                s, v = done(t)
                pe.wait_ge(s, v)
                if t >= 2:
                    pe.wait_ge(s_mod, t - 1)
                for j in range(KT):
                    i = pe.transpose(k.bank[4 + 2 * (t % 2) + j // 4][:, (j % 4) * P:(j % 4 + 1) * P], final(t)[:, j * P:(j + 1) * P], k.ident[:, :])
                i.then_inc(s_tr, 1)

            for t in range(tiles):
                if kind == 1:
                    if t >= 2:
                        pe.wait_ge(s_dve, C * (t - 2) + 1)
                    for kt in range(KT):
                        if t == 0:
                            pe.wait_ge(s_low, kt + 1)
                        if kt == 0:
                            pe.wait_ge(s_low, NW + t + 1)
                        for half in range(2):
                            n = slice(half * 512, half * 512 + 512)
                            o = k.bank[2 * (t % 2) + half][:, :]
                            pe.matmul(o, cath[:, t % 2, kt, :], wh[:, kt, n], start=kt == 0, stop=False)
                            pe.matmul(o, cath[:, t % 2, kt, :], wl[:, kt, n], start=False, stop=False)
                            i = pe.matmul(o, catl[:, t % 2, kt, :], wh[:, kt, n], start=False, stop=kt == KT - 1)
                    i.then_inc(s_yps, 1)
                if not last:
                    if kind == 1:
                        if t >= 1:
                            transposes(t - 1)
                    else:
                        transposes(t)
            if kind == 1:
                transposes(tiles - 1)


def stage_gating(nc, io, k):
    sb = Place(nc, "gate", k.after_ht)
    NU = 8
    wh, wl = sb("wh", [P, NU, KT, P], F32R), sb("wl", [P, NU, KT, P], F32R)
    raw = sb("raw", [P, 2, KT, P])
    wsr, wst = sb("wsr", [P, 8, P]), sb("wst", [P, 8, P])
    bsr, bst = sb("bsr", [8, P]), sb("bst", [P, 8])
    lng, lnb = sb("lng", [P, 512]), sb("lnb", [P, 512])
    gv, vn, uu, bo = [sb(x, [P, 2, 512]) for x in ("gv", "vn", "uu", "bo")]
    bot = sb("bot", [P, 2, 4, P])
    stats, mv, rstd = sb("stats", [P, 2, 6]), sb("mv", [P, 2, 2]), sb("rstd", [P, 2, 2])
    sem = lambda n: k.sem(f"gate_{n}")
    s_in, s_skew = sem("in"), sem("skew")
    s_raw = [sem("raw0"), sem("raw1")]
    s_high, s_low, s_wst, s_wsc = sem("high"), sem("low"), sem("wst"), sem("wsc")
    s_gv, s_u, s_gelu, s_gelu_u, s_dve, s_std, s_ln, s_mix, s_bo, s_bt, s_bc = [sem(x) for x in (
        "gv", "u", "gelu", "gelu_u", "dve", "std", "ln", "mix", "bo", "bt", "bc")]
    s_st = [sem("st0"), sem("st1")]
    T = XT + CT
    first = 768
    cols = [first + 512 + P * i for i in range(4)] + [first + P * i for i in range(4)]
    C = 4
    with nc.Block() as block:
        @block.sync
        def _(sp):
            sp.dma_start(wsr[:, :, :], io["b_ws"][0].rearrange("g p q -> p g q")).then_inc(s_in, 16)
            sp.dma_start(bsr[:, :], io["b_bs"][0]).then_inc(s_in, 16)
            sp.dma_start(lng[:, :], bass.AP(tensor=io["b_ln_g"].tensor, offset=0, ap=[[0, P], [1, 512]])).then_inc(s_in, 16)
            sp.dma_start(lnb[:, :], bass.AP(tensor=io["b_ln_b"].tensor, offset=0, ap=[[0, P], [1, 512]])).then_inc(s_in, 16)
            for u in range(NU):
                if u >= 2:
                    sp.wait_ge(s_low, u - 1)
                sp.dma_start(raw[:, u % 2, :, :], io["ab_w_in"][0].rearrange("(k p) n -> p k n", p=P)[:, :, cols[u]:cols[u] + P]
                             ).then_inc(s_raw[u % 2], 16)
            for h in range(16):
                sp.dma_start(k.skew_dram[h].rearrange("c r x -> r c x"),
                             bass.AP(tensor=k.rp_dram.tensor, offset=h * RP_ROWS * RP_W + 63,
                                     ap=[[RP_W, RP_ROWS], [-1, GRID_W], [1, GRID_W]])).then_inc(s_skew, 16)
            for t in range(T):
                sp.wait_ge(s_bc, t + 1)
                sp.dma_start(k.cat_dram.rearrange("(j p) t -> p j t", p=P)[:, 4:8, t * P:(t + 1) * P], bot[:, t % 2, :, :]).then_inc(s_st[t % 2], 16)
            for i in range(2):
                sp.wait_ge(s_st[i], 16 * (T // 2))
            sp.wait_ge(s_skew, 16 * 16)

        @block.scalar
        def _(act):
            for u in range(NU):
                act.wait_ge(s_raw[u % 2], 16 * (u // 2 + 1))
                act.activation(wh[:, u, :, :], raw[:, u % 2, :, :], ACT.Copy).then_inc(s_high, 1)
            for t in range(T + 1):
                if t < T:
                    act.wait_ge(s_gv, t + 1)
                    if t >= 2:
                        act.wait_ge(s_dve, C * (t - 2) + 4)
                    act.activation(gv[:, t % 2, :], k.bank[t % 2][:, :], ACT.Gelu).then_inc(s_gelu, 1)
                    act.wait_ge(s_u, t + 1)
                    if t >= 2:
                        act.wait_ge(s_bo, 2 * (t - 1))
                    act.activation(uu[:, t % 2, :], k.bank[2 + t % 2][:, :], ACT.Gelu).then_inc(s_gelu_u, 1)
                    act.wait_ge(s_dve, C * t + 2)
                    act.activation(rstd[:, t % 2, 0:1], mv[:, t % 2, 1:2], ACT.Sqrt, bias=k.eps[:, 0:1]).then_inc(s_std, 1)
                if t >= 1:
                    act.wait_ge(s_bt, t)
                    if t >= 3:
                        act.wait_ge(s_st[(t - 1) % 2], 16 * ((t - 1) // 2))
                    act.activation(bot[:, (t - 1) % 2, :, :], k.bank[7][:, :].rearrange("p (j q) -> p j q", q=P), ACT.Copy).then_inc(s_bc, 1)

        @block.gpsimd
        def _(pool):
            pool.wait_ge(s_in, 64)
            for t in range(T):
                v = vn[:, t % 2, :]
                pool.wait_ge(s_dve, C * t + 4)
                pool.tensor_tensor(v, v, lng[:, :], ALU.mult).then_inc(s_ln, 1)
                pool.wait_ge(s_ln, 2 * t + 1)
                pool.tensor_tensor(v, v, lnb[:, :], ALU.add).then_inc(s_ln, 1)

        @block.vector
        def _(dve):
            k.clear_last(dve)
            dve.wait_ge(s_wst, 1)
            for half in range(2):
                dve.tensor_copy(wst[:, 4 * half:4 * half + 4, :], k.bank[4 + half][:, :].rearrange("p (g q) -> p g q", q=P)).then_inc(s_wsc, 1)
            dve.tensor_copy(bst[:, :], k.bank[6][:, 0:8]).then_inc(s_wsc, 1)
            for u in range(NU):
                dve.wait_ge(s_high, u + 1)
                dve.tensor_tensor(wl[:, u, :, :], raw[:, u % 2, :, :], f32(wh[:, u, :, :]), ALU.subtract).then_inc(s_low, 1)

            def combine(t):
                dve.wait_ge(s_mix, t + 1)
                dve.wait_ge(s_wsc, 3)
                if t >= 2:
                    dve.wait_ge(s_bt, t - 1)
                dve.tensor_tensor(bo[:, t % 2, :].rearrange("p (g c) -> p g c", g=8),
                                  k.bank[4][:, :].rearrange("p (g c) -> p g c", g=8),
                                  bst[:, :].unsqueeze(2).broadcast_to([P, 8, 64]), ALU.add).then_inc(s_bo, 1)
                dve.wait_ge(s_bo, 2 * t + 1)
                dve.wait_ge(s_gelu_u, t + 1)
                dve.tensor_tensor(bo[:, t % 2, :], bo[:, t % 2, :], uu[:, t % 2, :], ALU.mult).then_inc(s_bo, 1)

            for t in range(T):
                n = C * t
                dve.wait_ge(s_gelu, t + 1)
                dve.bn_stats(stats[:, t % 2, :], gv[:, t % 2, :]).then_inc(s_dve, 1)
                dve.wait_ge(s_dve, n + 1)
                dve.bn_aggr(mv[:, t % 2, :], stats[:, t % 2, :]).then_inc(s_dve, 1)
                dve.wait_ge(s_std, t + 1)
                dve.reciprocal(rstd[:, t % 2, 1:2], rstd[:, t % 2, 0:1]).then_inc(s_dve, 1)
                dve.wait_ge(s_dve, n + 3)
                if t >= 2:
                    dve.wait_ge(s_mix, t - 1)
                dve.tensor_scalar(vn[:, t % 2, :], gv[:, t % 2, :], mv[:, t % 2, 0:1], rstd[:, t % 2, 1:2],
                                  ALU.subtract, ALU.mult).then_inc(s_dve, 1)
                if t >= 1:
                    combine(t - 1)
            combine(T - 1)

        @block.tensor
        def _(pe):
            pe.wait_ge(s_in, 64)
            for g in range(8):
                pe.transpose(k.bank[4 + g // 4][:, (g % 4) * P:(g % 4 + 1) * P], wsr[:, g, :], k.ident[:, :])
            pe.transpose(k.bank[6][:, 0:8], bsr[:, :], k.ident[0:8, 0:8]).then_inc(s_wst, 1)

            def mix(t):
                pe.wait_ge(s_ln, 2 * t + 2)
                pe.wait_ge(s_wsc, 3)
                if t >= 1:
                    pe.wait_ge(s_bo, 2 * t - 1)
                for g in range(8):
                    i = pe.matmul(k.bank[4][:, g * 64:(g + 1) * 64], wst[:, g, :], vn[:, t % 2, g * 64:(g + 1) * 64], start=True, stop=True)
                i.then_inc(s_mix, 1)

            def turn(t):
                pe.wait_ge(s_bo, 2 * t + 2)
                if t >= 1:
                    pe.wait_ge(s_bc, t)
                for j in range(4):
                    i = pe.transpose(k.bank[7][:, j * P:(j + 1) * P], bo[:, t % 2, j * P:(j + 1) * P], k.ident[:, :])
                i.then_inc(s_bt, 1)

            def product(t, u0, bank, done, free):
                if t >= 2:
                    pe.wait_ge(free, t - 1)
                for kt in range(KT):
                    if t == 0 and kt == 0:
                        pe.wait_ge(s_low, u0 + 4)
                    a, b = k.hth[:, kt, t * P:(t + 1) * P], k.htl[:, kt, t * P:(t + 1) * P]
                    h, lo = wh[:, u0:u0 + 4, kt, :], wl[:, u0:u0 + 4, kt, :]
                    pe.matmul(k.bank[bank][:, :], a, h, start=kt == 0, stop=False)
                    pe.matmul(k.bank[bank][:, :], a, lo, start=False, stop=False)
                    i = pe.matmul(k.bank[bank][:, :], b, h, start=False, stop=kt == KT - 1)
                i.then_inc(done, 1)

            for t in range(T):
                product(t, 0, t % 2, s_gv, s_gelu)
                if t >= 1:
                    mix(t - 1)
                product(t, 4, 2 + t % 2, s_u, s_gelu_u)
                if t >= 1:
                    turn(t - 1)
            mix(T - 1)
            turn(T - 1)


def stage_attention(nc, io, k, layer):
    L0 = layer == 0
    tag = f"a{layer}"
    sb = Place(nc, tag, k.after_ht)
    G = 4 if L0 else 8
    wq_h, wq_l, wk_h, wk_l, wv_h, wv_l = [sb(x, [P, KT, P], F32R) for x in ("wqh", "wql", "wkh", "wkl", "wvh", "wvl")]
    wh, wl = [wv_h, wk_h, wq_h], [wv_l, wk_l, wq_l]
    raw = sb("raw", [P, 3, KT, P])
    QT = TOK if L0 else SEQ
    qh, ql = sb("qh", [P, 2, QT], F32R), sb("ql", [P, 2, QT], F32R)
    kh, kl = sb("kh", [P, TOK], F32R), sb("kl", [P, TOK], F32R)
    vt, v = sb("vt", [P, TOK]), sb("v", [P, XT + CT, P])
    ao = sb("ao", [P, QT])
    LOC = 384 if L0 else 576
    sl = sb("sl", [P, 2, LOC])
    pr = sb("pr", [P, 2, LOC + CTX])
    NKT = (LOC + P - 1) // P + CT
    ptt = sb("ptt", [P, 2, NKT, P])
    small = sb("small", [P, 2, 8])
    if L0:
        rc, rs = sb("rc", [P, SEQ]), sb("rs", [P, SEQ])
        t1, t2, rot = sb("t1", [P, 512]), sb("t2", [P, 512]), sb("rot", [P, 512])
        band = sb("band", [P, LOC])
        sink, nsink = sb("sink", [P, 8]), sb("nsink", [P, 8])
    else:
        bias = sb("bias", [P, 2, 16, GRID_W])
        mid = sb("mid", [P, 2, 9, GRID_W])
        colm, rowm = sb("colm", [P, GRID_W]), sb("rowm", [P, 9, GRID_W])
    sem = lambda n: k.sem(f"{tag}_{n}")
    s_tab = sem("tab")
    s_raw = [sem("raw_v"), sem("raw_k"), sem("raw_q")]
    s_high, s_low = [sem(f"high_{x}") for x in "vkq"], [sem(f"low_{x}") for x in "vkq"]
    s_job, s_free, s_vt, s_vtr, s_v = sem("job"), sem("free"), sem("vt"), sem("vtr"), sem("v")
    s_jh, s_rot, s_ns = sem("jh"), sem("rot"), sem("ns")
    s_bias, s_bias_in = sem("bias"), sem("bias_in")
    s_qk, s_max, s_exp, s_r, s_p, s_t, s_pta, s_ptd, s_pv, s_o, s_st, s_c = [sem(x) for x in (
        "qk", "max", "exp", "r", "p", "t", "pta", "ptd", "pv", "o", "st", "chain")]

    qgroups, kgroups = groups_of(QT), groups_of(TOK)
    NK, NQ = len(kgroups), len(qgroups)
    PER = NQ if L0 else 2 * NK + NQ
    job_kv = lambda it: 0 if L0 else it * PER
    job_q = lambda it: 2 * NK + it * PER
    job_end = lambda it: 2 * NK + it * PER + NQ
    has_kv = lambda it: not L0 or (isinstance(it, int) and it == 0)
    units = []
    for hh in range(2):
        for t in range(QT // P):
            if L0:
                if t >= XT:
                    units.append((hh, t * P, 0, 0, None))
                else:
                    a, b = max(0, t - 1), min(XT, t + 2)
                    off = 0 if t else P
                    units.append((hh, t * P, a * P, (b - a) * P, band[:, off:off + (b - a) * P]))
            else:
                lo = min(max(2 * t - 4, 0), 8)
                rows = 9 if 2 <= t <= 5 else 8
                m = lo - 2 * t + 7
                tab = mid[:, hh, :, :] if rows == 9 else bias[:, hh, m:m + 8, :]
                units.append((hh, t * P, lo * GRID_W, rows * GRID_W, tab.rearrange("p r c -> p (r c)")))
    U = len(units)
    assert U % 2 == 0

    def ranges(nloc):
        if nloc == 0:
            return 0, []
        if nloc <= 384:
            return 0, [(0, 0, nloc)]
        at = 768 - nloc
        return at, [(at, 0, 512 - at), (512, 512 - at, 256)]

    w_in = io["ab_w_in"][0] if L0 else io["c_w_in"][0]
    w_view = w_in.rearrange("(k p) n -> p k n", p=P)

    def weight_dma(eng, which, it):
        dst, s = raw[:, which, :, :], s_raw[which]
        if L0:
            cols = [address(eng, it * HD + hh * 256) for hh in range(2)]
        else:
            cols = [address(eng, (2 - which) * D + it * P)]
        if not L0:
            col = cols[0]
            eng.dma_start(dst, w_view[:, :, bass.ds(col, P)]).then_inc(s, 16)
        elif which < 2:
            col = 512 + P * (1 - which)
            eng.dma_start(dst, w_view[:, :, col:col + P]).then_inc(s, 16)
        else:
            for hh in range(2):
                eng.dma_start(dst[:, :, hh * HD:(hh + 1) * HD], w_view[:, :, bass.ds(cols[hh], HD)]).then_inc(s, 16)

    TAB = 64 if L0 else 32
    RAWQ = 32 if L0 else 16
    kv_it = lambda it: 0 if L0 else it

    def over_groups(eng, body):
        body(0)
        with eng.Fori(1, G - 1) as it:
            body(it)
        body(G - 1)

    def is_last(it):
        return isinstance(it, int) and it == G - 1

    def nkt(u):
        return (units[u][3] + P - 1) // P + CT

    def bank_of(kind, j):
        return ({"v": 0, "k": NK, "q": 2 * NK}[kind] + j) % 4

    def rotated(kind, a):
        return L0 and a < SEQ

    def rot_count(it, kind, a):
        return 3 * ((0 if kind == "k" else 2 + 2 * it) + a // 512 + 1)

    def jh_count(it, kind, j):
        if L0:
            return j if kind == "k" else NK + NQ * it + j
        return (NK + NQ) * it + (j if kind == "k" else NK + j)

    def count_free(it, kind, j):
        return jh_count(it, kind, j)

    def ptd_count(it, u):
        per = sum(nkt(x) > 4 for x in range(U))
        return it * per + sum(nkt(x) > 4 for x in range(u))

    def free_before_q(it, j):
        return jh_count(it, "k", 0) + j if has_kv(it) and j else 0

    with nc.Block() as block:
        @block.sync
        def _(sp):
            if L0:
                sp.dma_start(rc[:, :], io["rope_c"]).then_inc(s_tab, 16)
                sp.dma_start(rs[:, :], io["rope_s"]).then_inc(s_tab, 16)
                sp.dma_start(band[:, :], io["band"]).then_inc(s_tab, 16)
                sp.dma_start(sink[:, :], bass.AP(tensor=io["a_sink"].tensor, offset=0, ap=[[0, P], [1, 8]])).then_inc(s_tab, 16)
            else:
                sp.dma_start(colm[:, :], io["colm"]).then_inc(s_tab, 16)
                sp.dma_start(rowm[:, :, :].rearrange("p r c -> p (r c)"), io["rowm"]).then_inc(s_tab, 16)

            def group(it):
                if isinstance(it, int) and it == 0:
                    for which in range(3):
                        weight_dma(sp, which, 0)
                if not L0:
                    heads = [address(sp, it * 2 + hh) for hh in range(2)]
                    wait(sp, s_max, U * it)
                    for hh in range(2):
                        for rr in range(2):
                            sp.dma_start(bias[rr * 64:rr * 64 + 64, hh, :, :],
                                         k.skew_dram[bass.ds(heads[hh], 1), :, 1 - rr:17 - rr, :].rearrange("h c r x -> c (h r) x")
                                         ).then_inc(s_bias_in, 16)
                if not is_last(it):
                    slices = (2,) if L0 else (0, 1, 2)
                    for which in slices:
                        wait(sp, s_low[which], it + 1)
                    for which in slices:
                        weight_dma(sp, which, it + 1)
                rows = [address(sp, it * HD + hh * 256) for hh in range(2)] if L0 else [address(sp, it * P)]
                wait(sp, s_o, U * (it + 1))
                if L0:
                    for hh in range(2):
                        sp.dma_start(k.cat_dram[bass.ds(rows[hh], HD), 0:QT], ao[hh * HD:(hh + 1) * HD, :]).then_inc(s_st, 16)
                else:
                    sp.dma_start(k.cat_dram[bass.ds(rows[0], P), 0:QT], ao[:, :]).then_inc(s_st, 16)
            over_groups(sp, group)
            sp.wait_ge(s_st, RAWQ * G)

        @block.gpsimd
        def _(pool):
            pool.wait_ge(s_tab, TAB)

            def group(it):
                wait(pool, s_bias_in, 64 * (it + 1))
                wait(pool, s_max, U * it)
                for hh in range(2):
                    b = bias[:, hh, :, :]
                    pool.tensor_tensor(b, b, colm[:, :].unsqueeze(1).broadcast_to([P, 16, GRID_W]), ALU.add).then_inc(s_bias, 1)
                wait(pool, s_bias, 4 * it + 2)
                for hh in range(2):
                    pool.tensor_tensor(mid[:, hh, :, :], bias[:, hh, 3:12, :], rowm[:, :, :], ALU.add).then_inc(s_bias, 1)
            if not L0:
                over_groups(pool, group)

        @block.scalar
        def _(act):
            def split(which, it):
                c = it if which == 2 else kv_it(it)
                wait(act, s_raw[which], (RAWQ if which == 2 else 16) * (c + 1))
                if not (isinstance(it, int) and it == 0):
                    wait(act, s_job, job_end(it - 1))
                src, dst = raw[:, which, :, :], wh[which][:, :, :]
                if L0 and which:
                    src = src.rearrange("p k (h i e) -> p (k h) e i", h=2, e=2)
                    dst = dst.rearrange("p k (h e i) -> p (k h) e i", h=2, e=2)
                    for e in range(2):
                        i = act.activation(dst[:, :, e, :], src[:, :, e, :], ACT.Copy)
                    i.then_inc(s_high[which], 1)
                else:
                    act.activation(dst, src, ACT.Copy).then_inc(s_high[which], 1)

            def parts(it, j, kind, a, n):
                x = k.bank[bank_of(kind, j)][:, 0:n]
                if rotated(kind, a):
                    wait(act, s_rot, rot_count(it, kind, a))
                    x = rot[:, 0:n]
                if kind == "k":
                    act.activation(kh[:, a:a + n], x, ACT.Copy).then_inc(s_jh, 1)
                else:
                    for hh in range(2):
                        i = act.activation(qh[:, hh, a:a + n], x, ACT.Identity, scale=k.sel[:, hh:hh + 1])
                    i.then_inc(s_jh, 1)

            def exps(it, u):
                hh, q0, k0, nloc, _ = units[u]
                n = it * U + u
                b = u % 2
                sm = small[:, b, :]
                wait(act, s_max, n + 1)
                wait(act, s_t, n - 1)
                p = pr[:, b, :]
                c = act.activation(p[:, nloc:nloc + CTX], k.bank[2 * b + 1][:, 256:512], ACT.Exp, bias=sm[:, 2:3],
                                   accum_out=sm[:, 4:5])
                if nloc:
                    c = act.activation(p[:, 0:nloc], sl[:, b, 0:nloc], ACT.Exp, bias=sm[:, 2:3], accum_out=sm[:, 3:4])
                if L0:
                    head = hh * 4 + it
                    c = act.activation(sm[:, 5:6], sink[:, bass.ds(head, 1)], ACT.Exp, bias=sm[:, 2:3])
                c.then_inc(s_exp, 1)

            def turned(it, u):
                n = it * U + u
                kts = nkt(u)
                m = min(4, kts)
                wait(act, s_t, n + 1)
                wait(act, s_pv, n - 1)
                act.activation(ptt[:, u % 2, 0:m, :], k.bank[4][:, 0:m * P].rearrange("p (j q) -> p j q", q=P), ACT.Copy).then_inc(s_pta, 1)

            def group(it):
                if isinstance(it, int) and it == 0:
                    for which in range(3):
                        split(which, 0)
                if has_kv(it):
                    for j, (a, n) in enumerate(kgroups):
                        wait(act, s_job, job_kv(it) + j + 1)
                        act.activation(vt[:, a:a + n], k.bank[bank_of("v", j)][:, 0:n], ACT.Copy).then_inc(s_vt, 1)
                    for j, (a, n) in enumerate(kgroups):
                        wait(act, s_job, job_kv(it) + NK + j + 1)
                        parts(it, j, "k", a, n)
                for j, (a, n) in enumerate(qgroups):
                    wait(act, s_job, job_q(it) + j + 1)
                    parts(it, j, "q", a, n)
                for s in range(U + 3):
                    if 0 <= s - 2 < U:
                        turned(it, s - 2)
                    if s < U:
                        exps(it, s)
                    if s == U // 2 and not is_last(it):
                        for which in range(3):
                            if which == 2 or not L0:
                                split(which, it + 1)
            over_groups(act, group)


        @block.vector
        def _(dve):
            k.clear_last(dve)
            def split(which, it):
                c = it if which == 2 else kv_it(it)
                wait(dve, s_high[which], c + 1)
                src, dst, h = raw[:, which, :, :], wl[which][:, :, :], f32(wh[which][:, :, :])
                if L0 and which:
                    src = src.rearrange("p k (h i e) -> p (k h) e i", h=2, e=2)
                    dst = dst.rearrange("p k (h e i) -> p (k h) e i", h=2, e=2)
                    h = h.rearrange("p k (h e i) -> p (k h) e i", h=2, e=2)
                    for e in range(2):
                        i = dve.tensor_tensor(dst[:, :, e, :], src[:, :, e, :], h[:, :, e, :], ALU.subtract)
                    i.then_inc(s_low[which], 1)
                else:
                    dve.tensor_tensor(dst, src, h, ALU.subtract).then_inc(s_low[which], 1)

            def parts(it, j, kind, a, n, count):
                x = k.bank[bank_of(kind, j)][:, 0:n]
                if rotated(kind, a):
                    c = rot_count(it, kind, a) - 3
                    wait(dve, s_jh, count)
                    wait(dve, s_free, count_free(it, kind, j))
                    dve.tensor_tensor(t1[:, 0:n], x, rc[:, a:a + n], ALU.mult).then_inc(s_rot, 1)
                    for qd in range(4):
                        o = 32 * (qd ^ 1)
                        i = dve.tensor_tensor(t2[o:o + 32, 0:n], x[32 * qd:32 * qd + 32, :], rs[32 * qd:32 * qd + 32, a:a + n], ALU.mult)
                    i.then_inc(s_rot, 1)
                    wait(dve, s_rot, c + 2)
                    dve.tensor_tensor(rot[:, 0:n], t1[:, 0:n], t2[:, 0:n], ALU.add).then_inc(s_rot, 1)
                    wait(dve, s_rot, c + 3)
                    x = rot[:, 0:n]
                wait(dve, s_jh, count + 1)
                if kind == "k":
                    dve.tensor_tensor(kl[:, a:a + n], x, f32(kh[:, a:a + n]), ALU.subtract).then_inc(s_free, 1)
                else:
                    for hh in range(2):
                        i = dve.scalar_tensor_tensor(out=ql[:, hh, a:a + n], in0=x, scalar=k.sel[:, hh:hh + 1],
                                                     in1=f32(qh[:, hh, a:a + n]), op0=ALU.mult, op1=ALU.subtract)
                    i.then_inc(s_free, 1)

            def maxima(it, u):
                hh, q0, k0, nloc, tab = units[u]
                n = it * U + u
                b = u % 2
                sm = small[:, b, :]
                wait(dve, s_qk, n + 1)
                wait(dve, s_exp, n - 1)
                wait(dve, s_p, n - 1)
                at, pieces = ranges(nloc)
                two = k.pair[b]
                c = dve.tensor_reduce(sm[:, 1:2], two[:, 768:1024], AXX, ALU.max, negate=True)
                if nloc:
                    c = dve.tensor_tensor_reduce(sl[:, b, 0:nloc], two[:, at:at + nloc], tab, 1.0, -3.0e38, ALU.add, ALU.max,
                                                 sm[:, 0:1])
                c.then_inc(s_c, 1)
                wait(dve, s_c, before_maxima(n, u) + 1)
                if L0:
                    head = hh * 4 + it
                    ns = nsink[:, bass.ds(head, 1)]
                    if nloc:
                        dve.scalar_tensor_tensor(out=sm[:, 6:7], in0=sm[:, 0:1], scalar=-1.0, in1=sm[:, 1:2], op0=ALU.mult,
                                                 op1=ALU.min).then_inc(s_c, 1)
                    else:
                        dve.tensor_copy(sm[:, 6:7], sm[:, 1:2]).then_inc(s_c, 1)
                    wait(dve, s_c, before_maxima(n, u) + 2)
                    dve.tensor_tensor(sm[:, 2:3], sm[:, 6:7], ns, ALU.min).then_inc(s_max, 1)
                else:
                    dve.scalar_tensor_tensor(out=sm[:, 2:3], in0=sm[:, 0:1], scalar=-1.0, in1=sm[:, 1:2], op0=ALU.mult,
                                             op1=ALU.min).then_inc(s_max, 1)

            half = 2 if L0 else 1

            def sums(it, u):
                nloc = units[u][3]
                n = it * U + u
                sm = small[:, u % 2, :]
                wait(dve, s_exp, n + 1)
                if L0:
                    if nloc:
                        dve.tensor_tensor(sm[:, 6:7], sm[:, 3:4], sm[:, 4:5], ALU.add).then_inc(s_c, 1)
                    else:
                        dve.tensor_copy(sm[:, 6:7], sm[:, 4:5]).then_inc(s_c, 1)
                    wait(dve, s_c, before_sums(n, u) + 1)
                    dve.tensor_tensor(sm[:, 0:1], sm[:, 6:7], sm[:, 5:6], ALU.add).then_inc(s_c, 1)
                    wait(dve, s_c, before_sums(n, u) + 2)
                    dve.reciprocal(sm[:, 7:8], sm[:, 0:1]).then_inc(s_r, 1)
                else:
                    dve.tensor_tensor(sm[:, 6:7], sm[:, 3:4], sm[:, 4:5], ALU.add).then_inc(s_c, 1)
                    wait(dve, s_c, before_sums(n, u) + 1)
                    dve.reciprocal(sm[:, 7:8], sm[:, 6:7]).then_inc(s_r, 1)
                wait(dve, s_r, n + 1)
                p = pr[:, u % 2, 0:nloc + CTX]
                dve.tensor_scalar(p, p, sm[:, 7:8], None, ALU.mult).then_inc(s_p, 1)

            def before_maxima(n, u):
                return half * (2 * n - 1) if u else half * 2 * n

            def before_sums(n, u):
                return half * (2 * n + 2) if u < U - 1 else half * (2 * n + 1)

            def turned(it, u):
                n = it * U + u
                kts = nkt(u)
                if kts > 4:
                    wait(dve, s_t, n + 1)
                    wait(dve, s_pv, n - 1)
                    dve.tensor_copy(ptt[:, u % 2, 4:kts, :], k.bank[5][:, 0:(kts - 4) * P].rearrange("p (j q) -> p j q", q=P)).then_inc(s_ptd, 1)

            def heads_out(it, u):
                hh, q0, _, _, _ = units[u]
                n = it * U + u
                wait(dve, s_pv, n + 1)
                if u == 0:
                    wait(dve, s_st, RAWQ * it)
                rows = slice(hh * HD, (hh + 1) * HD)
                dve.tensor_copy(ao[rows, q0:q0 + P], k.bank[6 + u % 2][rows, 0:P]).then_inc(s_o, 1)

            def group(it):
                if isinstance(it, int) and it == 0:
                    wait(dve, s_tab, TAB)
                    if L0:
                        dve.tensor_scalar(nsink[:, :], sink[:, :], -1.0, None, ALU.mult).then_inc(s_ns, 1)
                        wait(dve, s_ns, 1)
                    for which in range(3):
                        split(which, 0)
                if has_kv(it):
                    for j, (a, n) in enumerate(kgroups):
                        wait(dve, s_job, job_kv(it) + NK + j + 1)
                        parts(it, j, "k", a, n, jh_count(it, "k", j))
                    for i, (t0, m) in enumerate(((0, 4), (4, 4), (8, 2))):
                        wait(dve, s_vtr, 3 * kv_it(it) + i + 1)
                        dve.tensor_copy(v[:, t0:t0 + m, :], k.bank[4 + i][:, 0:m * P].rearrange("p (j q) -> p j q", q=P)).then_inc(s_v, 1)
                for j, (a, n) in enumerate(qgroups):
                    wait(dve, s_job, job_q(it) + j + 1)
                    parts(it, j, "q", a, n, jh_count(it, "q", j))
                if not L0:
                    wait(dve, s_bias, 4 * it + 4)
                for s in range(U + 3):
                    if s < U:
                        maxima(it, s)
                    if 0 <= s - 1 < U:
                        sums(it, s - 1)
                    if 0 <= s - 2 < U:
                        turned(it, s - 2)
                    if 0 <= s - 3 < U:
                        heads_out(it, s - 3)
                    if s == U // 2 and not is_last(it):
                        for which in range(3):
                            if which == 2 or not L0:
                                split(which, it + 1)

            over_groups(dve, group)


        @block.tensor
        def _(pe):
            def job(it, which, kind, j, a, n):
                b = bank_of(kind, j)
                first = j == 0
                if first:
                    c = it if which == 2 else kv_it(it)
                    wait(pe, s_low[which], c + 1)
                o = k.bank[b][:, 0:n]
                for kt in range(KT):
                    mv_h, mv_l = k.hth[:, kt, a:a + n], k.htl[:, kt, a:a + n]
                    pe.matmul(o, wh[which][:, kt, :], mv_h, start=kt == 0, stop=False)
                    pe.matmul(o, wh[which][:, kt, :], mv_l, start=False, stop=False)
                    i = pe.matmul(o, wl[which][:, kt, :], mv_h, start=False, stop=kt == KT - 1)
                i.then_inc(s_job, 1)

            def scores(it, u):
                hh, q0, k0, nloc, _ = units[u]
                n = it * U + u
                b = u % 2
                wait(pe, s_exp, n - 1)
                qs = slice(q0, q0 + P)
                at, pieces = ranges(nloc)
                two = k.pair[b]
                for c, kk, m in [(c, k0 + kk, m) for c, kk, m in pieces] + [(768, SEQ, CTX)]:
                    o = two[:, c:c + m]
                    pe.matmul(o, qh[:, hh, qs], kh[:, kk:kk + m], start=True, stop=False)
                    pe.matmul(o, qh[:, hh, qs], kl[:, kk:kk + m], start=False, stop=False)
                    i = pe.matmul(o, ql[:, hh, qs], kh[:, kk:kk + m], start=False, stop=True)
                i.then_inc(s_qk, 1)

            def key_tiles(u):
                hh, q0, k0, nloc, _ = units[u]
                loc = [(c, min(P, nloc - c), (k0 + c) // P) for c in range(0, nloc, P)]
                return loc + [(nloc + c * P, P, XT + c) for c in range(CT)]

            def turn(it, u):
                n = it * U + u
                wait(pe, s_p, n + 1)
                wait(pe, s_pta, n)
                wait(pe, s_ptd, ptd_count(it, u))
                for j, (c, m, _) in enumerate(key_tiles(u)):
                    i = pe.transpose(k.bank[4 + j // 4][0:m, (j % 4) * P:(j % 4 + 1) * P], pr[:, u % 2, c:c + m], k.ident[:, :])
                i.then_inc(s_t, 1)

            def values(it, u):
                hh = units[u][0]
                n = it * U + u
                wait(pe, s_pta, n + 1)
                wait(pe, s_ptd, ptd_count(it, u + 1))
                wait(pe, s_o, n - 1)
                kts = key_tiles(u)
                o = k.bank[6 + u % 2][hh * HD:(hh + 1) * HD, 0:P]
                for j, (c, m, t) in enumerate(kts):
                    i = pe.matmul(o, v[0:m, t, hh * HD:(hh + 1) * HD], ptt[0:m, u % 2, j, :], start=j == 0, stop=j == len(kts) - 1)
                i.then_inc(s_pv, 1)

            def group(it):
                wait(pe, s_exp, U * it)
                if has_kv(it):
                    for which, kind in ((0, "v"), (1, "k")):
                        for j, (a, n) in enumerate(kgroups):
                            if kind == "k" and j >= 1:
                                wait(pe, s_vt, NK * kv_it(it) + j)
                            job(it, which, kind, j, a, n)
                    wait(pe, s_ptd, ptd_count(it, 0))
                    wait(pe, s_pta, U * it)
                    wait(pe, s_vt, NK * (kv_it(it) + 1))
                    wait(pe, s_o, U * it)
                    for i0, (t0, m) in enumerate(((0, 4), (4, 4), (8, 2))):
                        for j in range(m):
                            i = pe.transpose(k.bank[4 + i0][:, j * P:(j + 1) * P], vt[:, (t0 + j) * P:(t0 + j + 1) * P], k.ident[:, :])
                        i.then_inc(s_vtr, 1)
                for j, (a, n) in enumerate(qgroups):
                    wait(pe, s_free, free_before_q(it, j))
                    job(it, 2, "q", j, a, n)
                wait(pe, s_free, jh_count(it, "q", NQ - 1) + 1)
                wait(pe, s_v, 3 * (kv_it(it) + 1))
                for s in range(U + 3):
                    if s < U:
                        scores(it, s)
                    if 0 <= s - 2 < U:
                        turn(it, s - 2)
                    if 0 <= s - 3 < U:
                        values(it, s - 3)
            over_groups(pe, group)


def stage_mlp(nc, io, k, layer):
    tag = f"m{layer}"
    sb = Place(nc, tag, k.after_y)
    tiles = XT + CT if layer == 0 else XT
    groups = groups_of(tiles * P)
    NG, M = len(groups), FC // P
    J = NG * M
    NB1 = 3 if J % 3 == 0 else 4
    wah, wal = sb("wah", [P, M, KT, P], F32R), sb("wal", [P, M, KT, P], F32R)
    wbh, wbl = sb("wbh", [P, M, D], F32R), sb("wbl", [P, M, D], F32R)
    rawa, rawb = sb("rawa", [P, M, KT, P]), sb("rawb", [P, M, D])
    ath, atl = sb("ath", [P, M, tiles * P], F32R), sb("atl", [P, M, tiles * P], F32R)
    rel, sq = sb("rel", [P, 2, 512]), sb("sq", [P, 2, 512])
    sem = lambda n: k.sem(f"{tag}_{n}")
    s_rawa, s_rawb = [sem(f"rawa{i}") for i in range(M)], [sem(f"rawb{i}") for i in range(M)]
    s_ahigh, s_alow, s_bhigh, s_blow = sem("ahigh"), sem("alow"), sem("bhigh"), sem("blow")
    s_h, s_relu, s_sq, s_ath, s_atl, s_w2, s_y = [sem(x) for x in ("h", "relu", "sq", "ath", "atl", "w2", "y")]
    w1 = io["mlp_w1"][layer].rearrange("(k p) f -> p k f", p=P)
    w2 = io["mlp_w2"][layer]
    tiles_of = lambda g: range(groups[g][0] // P, (groups[g][0] + groups[g][1]) // P)

    def over_steps(eng, body):
        body(0)
        with eng.Fori(1, NCH) as c:
            body(c)

    with nc.Block() as block:
        @block.sync
        def _(sp):
            def step(c):
                for m in range(M):
                    at = address(sp, c * FC + m * P)
                    wait(sp, s_alow, M * (c - 1) + m + 1)
                    sp.dma_start(rawa[:, m, :, :], w1[:, :, bass.ds(at, P)]).then_inc(s_rawa[m], 16)
                for m in range(M):
                    at = address(sp, c * FC + m * P)
                    wait(sp, s_blow, M * (c - 1) + m + 1)
                    sp.dma_start(rawb[:, m, :], w2[bass.ds(at, P), :]).then_inc(s_rawb[m], 16)
            over_steps(sp, step)

        @block.scalar
        def _(act):
            def step(c):
                for m in range(M):
                    wait(act, s_rawa[m], 16 * (c + 1))
                    wait(act, s_h, J * c)
                    act.activation(wah[:, m, :, :], rawa[:, m, :, :], ACT.Copy).then_inc(s_ahigh, 1)
                for g, (a, n) in enumerate(groups):
                    if g == NG - 1:
                        for m in range(M):
                            wait(act, s_rawb[m], 16 * (c + 1))
                            wait(act, s_w2, tiles * c)
                            act.activation(wbh[:, m, :], rawb[:, m, :], ACT.Copy).then_inc(s_bhigh, 1)
                    for m in range(M):
                        j = J * c + g * M + m
                        jj = g * M + m
                        wait(act, s_h, j + 1)
                        wait(act, s_sq, j - 1)
                        wait(act, s_ath, j - 1)
                        act.activation(rel[:, m % 2, 0:n], k.bank[4 + jj % NB1][:, 0:n], ACT.Relu).then_inc(s_relu, 1)
                        wait(act, s_relu, j + 1)
                        act.activation(ath[:, m, a:a + n], rel[:, m % 2, 0:n], ACT.Square).then_inc(s_ath, 1)
            over_steps(act, step)

        @block.gpsimd
        def _(pool):
            def step(c):
                for m in range(M):
                    wait(pool, s_ahigh, M * c + m + 1)
                    pool.tensor_tensor(wal[:, m, :, :], rawa[:, m, :, :], f32(wah[:, m, :, :]), ALU.subtract).then_inc(s_alow, 1)
                for g, (a, n) in enumerate(groups):
                    for m in range(M):
                        j = J * c + g * M + m
                        wait(pool, s_relu, j + 1)
                        wait(pool, s_atl, j - 1)
                        r = rel[:, m % 2, 0:n]
                        pool.tensor_tensor(sq[:, m % 2, 0:n], r, r, ALU.mult).then_inc(s_sq, 1)
            over_steps(pool, step)

        @block.vector
        def _(dve):
            k.clear_last(dve)
            def sums(c, g):
                for t in tiles_of(g):
                    n = tiles * c + t
                    wait(dve, s_w2, n + 1)
                    wait(dve, s_y, n + 1)
                    dve.tensor_tensor(k.y[:, t, :], k.y[:, t, :], k.pair[t % 2][:, :], ALU.add).then_inc(s_y, 1)

            def step(c):
                for g, (a, n) in enumerate(groups):
                    if not (isinstance(c, int) and c == 0):
                        sums(c - 1, g)
                    if g == NG - 1:
                        for m in range(M):
                            wait(dve, s_bhigh, M * c + m + 1)
                            dve.tensor_tensor(wbl[:, m, :], rawb[:, m, :], f32(wbh[:, m, :]), ALU.subtract).then_inc(s_blow, 1)
                    for m in range(M):
                        j = J * c + g * M + m
                        wait(dve, s_sq, j + 1)
                        wait(dve, s_ath, j + 1)
                        dve.tensor_tensor(atl[:, m, a:a + n], sq[:, m % 2, 0:n], f32(ath[:, m, a:a + n]), ALU.subtract).then_inc(s_atl, 1)
            for t in range(tiles):
                dve.memset(k.y[:, t, :], 0.0).then_inc(s_y, 1)
            over_steps(dve, step)
            for g in range(NG):
                sums(NCH - 1, g)

        @block.tensor
        def _(pe):
            def second(c, g):
                for t in tiles_of(g):
                    n = tiles * c + t
                    wait(pe, s_y, tiles + n - 1)
                    wait(pe, s_atl, J * c + M * (g + 1))
                    wait(pe, s_blow, M * (c + 1))
                    ts = slice(t * P, t * P + P)
                    for half in range(2):
                        o, cols = k.bank[2 * (t % 2) + half][:, :], slice(half * 512, half * 512 + 512)
                        for m in range(M):
                            pe.matmul(o, ath[:, m, ts], wbh[:, m, cols], start=m == 0, stop=False)
                            pe.matmul(o, ath[:, m, ts], wbl[:, m, cols], start=False, stop=False)
                            i = pe.matmul(o, atl[:, m, ts], wbh[:, m, cols], start=False, stop=m == M - 1)
                    i.then_inc(s_w2, 1)

            def step(c):
                for g, (a, n) in enumerate(groups):
                    if not (isinstance(c, int) and c == 0):
                        second(c - 1, g)
                    for m in range(M):
                        jj = g * M + m
                        wait(pe, s_alow, M * c + m + 1)
                        wait(pe, s_relu, J * c + jj + 1 - NB1)
                        o = k.bank[4 + jj % NB1][:, 0:n]
                        for kt in range(KT):
                            xh, xl = k.hth[:, kt, a:a + n], k.htl[:, kt, a:a + n]
                            pe.matmul(o, wah[:, m, kt, :], xh, start=kt == 0, stop=False)
                            pe.matmul(o, wah[:, m, kt, :], xl, start=False, stop=False)
                            i = pe.matmul(o, wal[:, m, kt, :], xh, start=False, stop=kt == KT - 1)
                        i.then_inc(s_h, 1)
            over_steps(pe, step)
            for g in range(NG):
                second(NCH - 1, g)


def constants():
    out = {"ident": np.eye(P, dtype=np.float32)}
    tok = np.arange(SEQ)
    n_pairs = HD // 4
    freqs = (np.float32(10000.0) ** (-np.arange(n_pairs, dtype=np.float32) / n_pairs)).astype(np.float32)
    row, col = (tok // GRID_W).astype(np.float32), (tok % GRID_W).astype(np.float32)
    ang = np.concatenate([row[:, None] * freqs, col[:, None] * freqs], axis=-1).astype(np.float32)
    cos, sin = np.cos(ang).T, np.sin(ang).T
    out["rope_c"] = np.ascontiguousarray(np.tile(cos, (4, 1))).astype(np.float32)
    out["rope_s"] = np.ascontiguousarray(np.concatenate([sin, -sin, sin, -sin])).astype(np.float32)
    i, j = np.arange(P)[:, None], np.arange(P)[None, :]
    z = np.zeros((P, P))
    out["band"] = np.concatenate([np.where(j >= i, 0, NEG), z, np.where(j <= i, 0, NEG)], axis=1).astype(np.float32)
    c, c2 = np.arange(P)[:, None] % GRID_W, np.arange(GRID_W)[None, :]
    start = np.clip(c - NA_COLS // 2, 0, GRID_W - NA_COLS)
    out["colm"] = np.where((c2 >= start) & (c2 < start + NA_COLS), 0, NEG).astype(np.float32)
    rowm = np.zeros((P, 9, GRID_W), np.float32)
    rowm[0:64, 8], rowm[64:, 0] = NEG, NEG
    out["rowm"] = rowm.reshape(P, -1)
    sel = np.zeros((P, 2), np.float32)
    sel[0:64, 0] = sel[64:, 1] = HD ** -0.5
    out["sel"] = sel
    out["eps"] = np.full((P, 1), EPS, np.float32)
    return out


def build(nc, io, out):
    k = Kept(nc)
    k.out = out
    at = 16512
    small = {}
    for name, shape in (("ident", [P, P]), ("sel", [P, 2]), ("eps", [P, 1]), ("mod", [P, 2, 48, 2])):
        small[name] = nc.alloc_sbuf_tensor_at(f"kept_{name}", shape, F32, offset=at)
        at += (int(np.prod(shape[1:])) * 4 + 31) // 32 * 32
    assert at <= BASE
    k.ident, k.sel, k.eps, k.mod = (small[x] for x in ("ident", "sel", "eps", "mod"))
    k.hth = nc.alloc_sbuf_tensor_at("hth", [P, KT, TOK], F32R, offset=BASE)
    k.htl = nc.alloc_sbuf_tensor_at("htl", [P, KT, TOK], F32R, offset=BASE + KT * TOK * 4)
    k.after_ht = BASE + 2 * KT * TOK * 4
    k.y = nc.alloc_sbuf_tensor_at("y", [P, XT + CT, D], F32, offset=k.after_ht)
    k.after_y = k.after_ht + (XT + CT) * D * 4
    pairs = [nc.alloc_psum_tensor(f"pair{i}", [P, 1024], F32) for i in range(4)]
    k.pair = pairs
    k.bank = [pairs[i // 2][:, (i % 2) * 512:(i % 2) * 512 + 512] for i in range(8)]
    k.x_dram = nc.dram_tensor("x_rows", [TOK, D], F32, kind="Internal").ap()
    k.cat_dram = nc.dram_tensor("cat_cols", [D, TOK], F32, kind="Internal").ap()
    k.gate_dram = nc.dram_tensor("gate_rows", [2, 2, 2 * KT, P], F32, kind="Internal").ap()
    k.skew_dram = nc.dram_tensor("skewed_rpb", [16, GRID_W, RP_ROWS, GRID_W], F32, kind="Internal").ap()
    k.rp_dram = nc.dram_tensor("padded_rpb", [16, RP_ROWS, RP_W], F32, kind="Internal").ap()
    stages = [(stage_modulation, ()), (stage_rows, (0, 0)), (stage_attention, (0,)), (stage_gating, ()), (stage_rows, (0, 1)),
              (stage_mlp, (0,)), (stage_rows, (0, 2)),
              (stage_attention, (1,)), (stage_rows, (1, 1)), (stage_mlp, (1,)), (stage_rows, (1, 2))]
    for stage, args in stages:
        stage(nc, io, k, *args)
        k.end_stage()


_INS = ["x", "c", "ctx", "c_ctx", "w_mod", "b_mod", "ab_w_in", "a_sink", "b_ln_g", "b_ln_b", "b_ws", "b_bs", "ab_w_out",
        "c_w_in", "c_rpb", "c_w_out", "ln1_g", "ln1_b", "mlp_w1", "mlp_w2", "ln2_g", "ln2_b"]


def kernel(**inputs):
    import concourse.bacc as bacc
    from concourse.bass_utils import run_bass_kernel_spmd

    nc = bacc.Bacc("TRN2", target_bir_lowering=False, num_devices=1)
    arrays, io = {}, {}
    for name in _INS:
        arrays[f"in_{name}"] = np.ascontiguousarray(inputs[name])
        io[name] = nc.dram_tensor(f"in_{name}", arrays[f"in_{name}"].shape, F32, kind="ExternalInput").ap()
    for name, a in constants().items():
        arrays[f"const_{name}"] = np.ascontiguousarray(a)
        io[name] = nc.dram_tensor(f"const_{name}", a.shape, F32, kind="ExternalInput").ap()
    out = nc.dram_tensor("out_x", (1, SEQ, D), F32, kind="ExternalOutput").ap()
    build(nc, io, out)
    r = run_bass_kernel_spmd(nc, [arrays], core_ids=[0])
    return r.results[0]["out_x"]
```

```python
import numpy as np
import concourse.bass as bass
from concourse import mybir

F32 = mybir.dt.float32
F32R = mybir.dt.float32r
ALU = mybir.AluOpType
ACT = mybir.ActivationFunctionType
AXX = mybir.AxisListType.X

P = 128
D = 1024
KT = D // P
SEQ, CTX = 1024, 256
TOK = SEQ + CTX
XT, CT = SEQ // P, CTX // P
DEPTH = 2
HD = 64
FF = 4 * D
FC = 256
NCH = FF // FC
ALPHA = (2 * DEPTH) ** 0.25
EPS = 1e-5
NEG = -1e30
GRID_W, NA_ROWS, NA_COLS = 64, 8, 16
RPB_R, RPB_C = 2 * NA_ROWS - 1, 2 * NA_COLS - 1
RP_ROWS, RP_W = RPB_R + 2, 128
SH_A, SC_A, G_A, SH_M, SC_M, G_M = range(6)

BASE = 20608
END = 229368


def wait(eng, sem, value):
    if isinstance(value, int) and value <= 0:
        return
    eng.wait_ge(sem, value)


def address(eng, value):
    return value if isinstance(value, int) else eng.snap(value)


class Place:

    def __init__(self, nc, tag, at=BASE):
        self.nc, self.tag, self.at = nc, tag, at

    def __call__(self, name, shape, dt=F32):
        size = int(np.prod(shape[1:])) * 4
        t = self.nc.alloc_sbuf_tensor_at(f"{self.tag}_{name}", shape, dt, offset=self.at)
        self.at += (size + 31) // 32 * 32
        assert self.at <= END, (self.tag, name, self.at)
        return t


class Kept:

    def __init__(self, nc):
        self.nc, self.live, self.dead = nc, [], []

    def sem(self, name):
        s = self.nc.alloc_semaphore(name)
        self.live.append(s)
        return s

    def clear_last(self, dve):
        for s in self.dead:
            dve.sem_clear(s)

    def end_stage(self):
        for s in self.dead:
            self.nc.release_semaphore(s)
        self.dead, self.live = self.live, []


def f32(ap):
    return ap.bitcast(F32)


def groups_of(tokens):
    return [(a, min(512, tokens - a)) for a in range(0, tokens, 512)]


def stage_modulation(nc, io, k):
    sb = Place(nc, "mod")
    PIECE = 512
    NB = 6 * D // PIECE
    RING = 6
    wbuf = sb("w", [P, RING, KT, PIECE])
    crow, csil, ccol = sb("crow", [2 * KT, P]), sb("csil", [2 * KT, P]), sb("ccol", [P, 2 * KT])
    brow = sb("brow", [2, 2, 6 * D])
    mrow = sb("mrow", [2, 3, PIECE])
    zero = sb("zero", [16, RP_ROWS, RP_W])
    s_const, s_in, s_pad, s_zero = k.sem("const"), k.sem("mod_in"), k.sem("mod_pad"), k.sem("mod_zero")
    s_w = [k.sem(f"mod_w{i}") for i in range(RING)]
    s_silu, s_tr, s_col, s_mm, s_add, s_turn, s_mod = [k.sem(f"mod_{x}") for x in ("silu", "tr", "col", "mm", "add", "turn", "mod")]
    s_gate = [k.sem(f"mod_gate{i}") for i in range(3)]
    N = 2 * NB
    part = lambda n: (n % NB) // 2
    gates = [n for n in range(N) if part(n) in (G_A, G_M)]
    turned = lambda n: k.bank[2 + n % 2]
    with nc.Block() as block:
        @block.sync
        def _(sp):
            for name, t in (("ident", k.ident), ("sel", k.sel), ("eps", k.eps)):
                sp.dma_start(t[:, :], io[name]).then_inc(s_const, 16)
            sp.dma_start(crow[0:KT, :], io["c"].rearrange("a (k p) -> (a k) p", p=P)).then_inc(s_in, 16)
            sp.dma_start(crow[KT:2 * KT, :], io["c_ctx"].rearrange("(k p) -> k p", p=P)).then_inc(s_in, 16)
            for c in range(2):
                sp.dma_start(brow[c:c + 1, :, :], io["b_mod"].rearrange("(a l) n -> a l n", a=1)).then_inc(s_in, 16)
            for n in range(N):
                if n >= RING:
                    sp.wait_ge(s_mm, n - RING + 1)
                src = io["w_mod"][n // NB].rearrange("(k p) n -> p k n", p=P)[:, :, (n % NB) * PIECE:(n % NB + 1) * PIECE]
                sp.dma_start(wbuf[:, n % RING, :, :], src).then_inc(s_w[n % RING], 16)
            sp.wait_ge(s_const, 48)

        @block.gpsimd
        def _(pool):
            pool.memset(zero[:, :, :], 0.0).then_inc(s_zero, 1)

        @block.scalar
        def _(act):
            act.wait_ge(s_in, 64)
            act.activation(csil[:, :], crow[:, :], ACT.Silu).then_inc(s_silu, 1)
            act.wait_ge(s_zero, 1)
            act.dma_start(k.rp_dram, zero[:, :, :]).then_inc(s_pad, 16)
            act.wait_ge(s_pad, 16)
            act.dma_start(k.rp_dram[:, 1:1 + RPB_R, 48:48 + RPB_C], io["c_rpb"][0]).then_inc(s_pad, 16)
            for n in gates:
                act.wait_ge(s_add, n + 1)
                g, j = 2 * (n // NB) + (part(n) == G_M), 4 * (n % 2)
                act.dma_start(k.gate_dram[g // 2, g % 2].rearrange("(j c) p -> c j p", c=2)[:, j:j + 4, :],
                              mrow[:, n % 3, :].rearrange("c (j p) -> c j p", p=P)).then_inc(s_gate[n % 3], 16)
            act.wait_ge(s_pad, 32)
            for i in range(3):
                act.wait_ge(s_gate[i], 16 * sum(n % 3 == i for n in gates))

        @block.tensor
        def _(pe):
            pe.wait_ge(s_silu, 1)
            pe.wait_ge(s_const, 48)
            pe.transpose(k.bank[0][:, 0:2 * KT], csil[:, :], k.ident[0:2 * KT, 0:2 * KT]).then_inc(s_tr, 1)
            pe.wait_ge(s_col, 1)

            def turn(n):
                pe.wait_ge(s_add, n + 1)
                if n >= 2:
                    pe.wait_ge(s_mod, n - 1)
                for j in range(4):
                    i = pe.transpose(turned(n)[:, 2 * j:2 * j + 2], mrow[:, n % 3, j * P:(j + 1) * P], k.ident[0:2, 0:2])
                i.then_inc(s_turn, 1)

            for n in range(N):
                pe.wait_ge(s_w[n % RING], 16 * (n // RING + 1))
                if n >= 2:
                    pe.wait_ge(s_add, n - 1)
                for kt in range(KT):
                    mm = pe.matmul(k.bank[n % 2][0:2, :], ccol[:, kt:2 * KT:KT], wbuf[:, n % RING, kt, :],
                                   start=kt == 0, stop=kt == KT - 1)
                mm.then_inc(s_mm, 1)
                if n >= 1:
                    turn(n - 1)
            turn(N - 1)

        @block.vector
        def _(dve):
            dve.wait_ge(s_tr, 1)
            dve.tensor_copy(ccol[:, :], k.bank[0][:, 0:2 * KT]).then_inc(s_col, 1)

            def columns(n):
                l, j = n // NB, 4 * (n % NB)
                dve.wait_ge(s_turn, n + 1)
                dve.tensor_scalar(k.mod[:, l, j:j + 4, :].rearrange("p j c -> p (j c)"), turned(n)[:, 0:8],
                                  1.0 if part(n) in (SC_A, SC_M) else 0.0, None, ALU.add).then_inc(s_mod, 1)

            for n in range(N):
                l, at = n // NB, (n % NB) * PIECE
                dve.wait_ge(s_mm, n + 1)
                if n >= 3:
                    dve.wait_ge(s_turn, n - 2)
                    if n - 3 in gates:
                        dve.wait_ge(s_gate[n % 3], 16 * sum(m % 3 == n % 3 for m in gates if m <= n - 3))
                dve.tensor_tensor(mrow[:, n % 3, :], k.bank[n % 2][0:2, :], brow[:, l, at:at + PIECE], ALU.add).then_inc(s_add, 1)
                if n >= 1:
                    columns(n - 1)
            columns(N - 1)


def stage_rows(nc, io, k, layer, kind):
    tag = f"r{layer}{kind}"
    sb = Place(nc, tag, k.after_ht)
    tiles = XT if (layer == DEPTH - 1 and kind) else XT + CT
    last = layer == DEPTH - 1 and kind == 2
    sem = lambda n: k.sem(f"{tag}_{n}")
    if kind == 2:
        y = k.y
        sb.at = k.after_y
    if kind == 1:
        wh, wl = sb("wh", [P, KT, D], F32R), sb("wl", [P, KT, D], F32R)
        raw = sb("raw", [P, 2, D])
        cath, catl = sb("cath", [P, 2, KT, P], F32R), sb("catl", [P, 2, KT, P], F32R)
    xbuf, mbuf, nbuf = (1, 1, 2) if kind == 1 else (3, 3, 4)
    shared = sb.at
    if kind < 2:
        xin = sb("xin", [P, xbuf, D])
    res = sb("res", [P, nbuf, D])
    modt = sb("modt", [P, mbuf, KT, P])
    if kind:
        lng, lnb = sb("lng", [P, D]), sb("lnb", [P, D])
    if kind == 2:
        rstd, nbias = sb("rstd", [P, 2, tiles]), sb("nbias", [P, tiles])
    if kind == 1:
        gate = sb("gate", [P, 2, D])
        stats, mv = sb("stats", [P, 2, 2, 6]), sb("mv", [P, 2, 2])
        rstd = sb("rstd", [P, 2, 2])
    if kind == 1:
        raww = nc.alloc_sbuf_tensor_at(f"{tag}_raww", [P, KT, D], F32, offset=shared)
        assert shared + KT * D * 4 <= sb.at
    s_row, s_x = sem("rows"), [sem(f"x{i}") for i in range(xbuf)]
    s_raw = [sem(f"raw{i}") for i in range(2)]
    s_raww = [sem(f"raww{i}") for i in range(KT if kind == 1 else 0)]
    s_whigh, s_wlow = sem("whigh"), sem("wlow")
    s_high, s_low, s_yps = sem("high"), sem("low"), sem("yps")
    s_dve, s_std, s_g, s_b, s_tr, s_mod, s_hh, s_hl = [sem(x) for x in ("dve", "std", "g", "b", "tr", "mod", "hh", "hl")]
    s_norm, s_odd = sem("norm"), sem("odd")
    s_store = [sem(f"store{i}") for i in range(nbuf)]
    next_layer, msh, msc = (layer, SH_M, SC_M) if kind == 1 else ((layer, SH_A, SC_A) if kind == 0 else (layer + 1, SH_A, SC_A))
    ln = 1 if kind == 1 else 2
    cond = lambda t: 0 if t < XT else 1
    src = lambda t: (io["x"][0] if t < XT else io["ctx"][0])[(t % XT) * P:(t % XT + 1) * P, :] if (layer == 0 and kind < 2) \
        else k.x_dram[t * P:(t + 1) * P, :]
    done = (lambda t: (s_b, t + 1)) if kind else (lambda t: (s_x[t % xbuf], 16 * (t // xbuf + 1)))
    final = lambda t: res[:, t % nbuf, :] if kind else xin[:, t % xbuf, :]
    C = 6

    with nc.Block() as block:
        @block.sync
        def _(sp):
            def cat_in(t):
                if t >= 2:
                    sp.wait_ge(s_low, t - 1)
                sp.dma_start(raw[:, t % 2, :].rearrange("p (j q) -> p j q", q=P),
                             k.cat_dram.rearrange("(j p) t -> p j t", p=P)[:, :, t * P:(t + 1) * P]).then_inc(s_raw[t % 2], 16)

            if kind == 1:
                w_out = io["ab_w_out" if layer == 0 else "c_w_out"][0]
                cat_in(0)
                for u in range(KT):
                    sp.dma_start(raww[:, u, :], w_out[u * P:(u + 1) * P, :]).then_inc(s_raww[u], 16)
                cat_in(1)
                sp.wait_ge(s_wlow, KT)
            if kind:
                sp.dma_start(lng[:, :], bass.AP(tensor=io[f"ln{ln}_g"].tensor, offset=layer * D, ap=[[0, P], [1, D]])).then_inc(s_row, 16)
                sp.dma_start(lnb[:, :], bass.AP(tensor=io[f"ln{ln}_b"].tensor, offset=layer * D, ap=[[0, P], [1, D]])).then_inc(s_row, 16)
            if kind == 1:
                for c in range(2):
                    at = (layer * 2 * 2 * KT + c) * P
                    sp.dma_start(gate[:, c, :].rearrange("p (j q) -> p j q", q=P),
                                 bass.AP(tensor=k.gate_dram.tensor, offset=at, ap=[[0, P], [2 * P, KT], [1, P]])).then_inc(s_row, 16)
            def residual_in(t):
                if t >= tiles or kind == 2:
                    return
                if t >= xbuf:
                    if kind:
                        sp.wait_ge(s_dve, C * (t - xbuf) + 2)
                    else:
                        sp.wait_ge(s_tr, t - xbuf + 1)
                sp.dma_start(xin[:, t % xbuf, :], src(t)).then_inc(s_x[t % xbuf], 16)

            for t in range(xbuf):
                residual_in(t)
            for t in range(tiles):
                if kind == 1 and t + 2 < tiles:
                    cat_in(t + 2)
                residual_in(t + xbuf)
                if kind:
                    sp.wait_ge(s_b, (t // 2 * 2 + 2) if last else t + 1)
                    dst = k.out[0, t * P:(t + 1) * P, :] if last else k.x_dram[t * P:(t + 1) * P, :]
                    sp.dma_start(dst, res[:, t % nbuf, :]).then_inc(s_store[t % nbuf], 16)
            if kind:
                for i in range(nbuf):
                    sp.wait_ge(s_store[i], 16 * len(range(i, tiles, nbuf)))

        @block.gpsimd
        def _(pool):
            if kind:
                pool.wait_ge(s_row, 64 if kind == 1 else 32)
            for t in range(0, tiles, 2 if last else 1):
                if last:
                    pool.wait_ge(s_norm, t + 1)
                    pool.tensor_tensor(res[:, t % nbuf, :], res[:, t % nbuf, :], lng[:, :], ALU.mult).then_inc(s_g, 1)
                elif kind == 2:
                    pool.wait_ge(s_dve, t + 2)
                    pool.tensor_tensor(res[:, t % nbuf, :], res[:, t % nbuf, :], lng[:, :], ALU.mult).then_inc(s_g, 1)
                elif kind == 1:
                    r = res[:, t % nbuf, :]
                    pool.wait_ge(s_dve, C * t + 6)
                    pool.tensor_tensor(r, r, lng[:, :], ALU.mult).then_inc(s_g, 1)
                    pool.wait_ge(s_g, t + 1)
                    pool.tensor_tensor(r, r, lnb[:, :], ALU.add).then_inc(s_b, 1)

        @block.scalar
        def _(act):
            def high(t):
                act.wait_ge(s_raw[t % 2], 16 * (t // 2 + 1))
                if t >= 2:
                    act.wait_ge(s_yps, t - 1)
                act.activation(cath[:, t % 2, :, :].rearrange("p j q -> p (j q)"), raw[:, t % 2, :], ACT.Copy).then_inc(s_high, 1)

            def modulate(t):
                act.wait_ge(s_tr, t + 1)
                if t >= mbuf:
                    act.wait_ge(s_hl, t - mbuf + 1)
                for j in range(KT):
                    col = lambda part: k.mod[:, next_layer, part * KT + j, cond(t):cond(t) + 1]
                    a = act.activation(modt[:, t % mbuf, j, :], k.bank[4 + 2 * (t % 2) + j // 4][:, (j % 4) * P:(j % 4 + 1) * P], ACT.Identity,
                                       scale=col(msc), bias=col(msh))
                a.then_inc(s_mod, 1)
                if kind:
                    act.wait_ge(s_mod, t + 1)
                if kind:
                    act.activation(k.hth[:, :, t * P:(t + 1) * P], modt[:, t % mbuf, :, :], ACT.Copy).then_inc(s_hh, 1)

            if kind == 1:
                high(0)
                for u in range(KT):
                    act.wait_ge(s_raww[u], 16)
                    act.activation(wh[:, u, :], raww[:, u, :], ACT.Copy).then_inc(s_whigh, 1)
            if kind == 2:
                act.activation(rstd[:, 0, :], k.mv[:, 0:tiles, 1], ACT.Sqrt, bias=k.eps[:, 0:1]).then_inc(s_std, 1)
            for t in range(tiles):
                if kind == 1 and t + 1 < tiles:
                    high(t + 1)
                if last:
                    if t == 0:
                        act.wait_ge(s_dve, 2)
                    if t >= nbuf:
                        act.wait_ge(s_store[t % nbuf], 16 * (t // nbuf))
                    act.activation(res[:, t % nbuf, :], y[:, t, :], ACT.Identity, scale=rstd[:, 1, t:t + 1],
                                   bias=nbias[:, t:t + 1]).then_inc(s_norm, 1)
                elif kind == 2:
                    modulate(t)
                elif kind == 1:
                    act.wait_ge(s_dve, C * t + 4)
                    act.activation(rstd[:, t % 2, 0:1], mv[:, t % 2, 1:2], ACT.Sqrt, bias=k.eps[:, 0:1]).then_inc(s_std, 1)
                    if t >= 1:
                        modulate(t - 1)
                else:
                    modulate(t)
            if kind == 1:
                modulate(tiles - 1)

        @block.vector
        def _(dve):
            k.clear_last(dve)
            def low(t):
                dve.wait_ge(s_high, t + 1)
                if t >= 2:
                    dve.wait_ge(s_yps, t - 1)
                dve.tensor_tensor(catl[:, t % 2, :, :].rearrange("p j q -> p (j q)"), raw[:, t % 2, :],
                                  f32(cath[:, t % 2, :, :].rearrange("p j q -> p (j q)")), ALU.subtract).then_inc(s_low, 1)

            def split_ht(t):
                if kind == 0:
                    dve.wait_ge(s_mod, t + 1)
                    dve.tensor_copy(k.hth[:, :, t * P:(t + 1) * P], modt[:, t % mbuf, :, :]).then_inc(s_hh, 1)
                dve.wait_ge(s_hh, t + 1)
                dve.tensor_tensor(k.htl[:, :, t * P:(t + 1) * P], modt[:, t % mbuf, :, :], f32(k.hth[:, :, t * P:(t + 1) * P]),
                                  ALU.subtract).then_inc(s_hl, 1)

            if kind == 1:
                low(0)
                for u in range(KT):
                    dve.wait_ge(s_whigh, u + 1)
                    dve.tensor_tensor(wl[:, u, :], raww[:, u, :], f32(wh[:, u, :]), ALU.subtract).then_inc(s_wlow, 1)
            if kind == 2:
                dve.wait_ge(s_row, 32)
                dve.wait_ge(s_std, 1)
                dve.reciprocal(rstd[:, 1, :], rstd[:, 0, :]).then_inc(s_dve, 1)
                dve.wait_ge(s_dve, 1)
                if last:
                    dve.scalar_tensor_tensor(out=nbias[:, :], in0=k.mv[:, 0:tiles, 0], scalar=-1.0, in1=rstd[:, 1, :],
                                             op0=ALU.mult, op1=ALU.mult).then_inc(s_dve, 1)
                    for t in [t ^ 1 for t in range(tiles)]:
                        r = res[:, t % nbuf, :]
                        if t % 2:
                            dve.wait_ge(s_norm, t + 1)
                            dve.tensor_tensor(r, r, lng[:, :], ALU.mult).then_inc(s_odd, 1)
                            dve.wait_ge(s_odd, t // 2 + 1)
                        else:
                            dve.wait_ge(s_g, t // 2 + 1)
                        dve.tensor_tensor(r, r, lnb[:, :], ALU.add).then_inc(s_b, 1)
                    return
                for t in range(tiles + 3):
                    if t < tiles:
                        if t >= nbuf:
                            dve.wait_ge(s_store[t % nbuf], 16 * (t // nbuf))
                            dve.wait_ge(s_tr, t - nbuf + 1)
                        dve.tensor_scalar(res[:, t % nbuf, :], y[:, t, :], k.mv[:, t, 0:1], rstd[:, 1, t:t + 1],
                                          ALU.subtract, ALU.mult).then_inc(s_dve, 1)
                    if 1 <= t <= tiles:
                        r = res[:, (t - 1) % nbuf, :]
                        dve.wait_ge(s_g, t)
                        dve.tensor_tensor(r, r, lnb[:, :], ALU.add).then_inc(s_b, 1)
                    if t >= 3:
                        split_ht(t - 3)
                return
            if kind == 1:
                dve.wait_ge(s_row, 64)
            for t in range(tiles):
                if kind == 1 and t + 1 < tiles:
                    low(t + 1)
                if kind:
                    n, r = C * t, res[:, t % nbuf, :]
                    if t >= nbuf:
                        dve.wait_ge(s_store[t % nbuf], 16 * (t // nbuf))
                        dve.wait_ge(s_tr, t - nbuf + 1)
                    g = gate[:, cond(t), :]
                    dve.wait_ge(s_yps, t + 1)
                    b = 2 * (t % 2)
                    for half in range(2):
                        i = dve.tensor_tensor(r[:, half * 512:half * 512 + 512], k.bank[b + half][:, :],
                                              g[:, half * 512:half * 512 + 512], ALU.mult)
                    i.then_inc(s_dve, 1)
                    dve.wait_ge(s_dve, n + 1)
                    dve.wait_ge(s_x[t % xbuf], 16 * (t // xbuf + 1))
                    dve.scalar_tensor_tensor(out=r, in0=xin[:, t % xbuf, :], scalar=ALPHA, in1=r, op0=ALU.mult,
                                             op1=ALU.add).then_inc(s_dve, 1)
                    dve.wait_ge(s_dve, n + 2)
                    for half in range(2):
                        i = dve.bn_stats(stats[:, t % 2, half, :], r[:, half * 512:half * 512 + 512])
                    i.then_inc(s_dve, 1)
                    dve.wait_ge(s_dve, n + 3)
                    dve.bn_aggr(mv[:, t % 2, :], stats[:, t % 2, :, :].rearrange("p a b -> p (a b)")).then_inc(s_dve, 1)
                    if t >= 2:
                        split_ht(t - 2)
                    dve.wait_ge(s_std, t + 1)
                    dve.reciprocal(rstd[:, t % 2, 1:2], rstd[:, t % 2, 0:1]).then_inc(s_dve, 1)
                    dve.wait_ge(s_dve, n + 5)
                    dve.tensor_scalar(r, r, mv[:, t % 2, 0:1], rstd[:, t % 2, 1:2], ALU.subtract, ALU.mult).then_inc(s_dve, 1)
                elif t >= 1:
                    split_ht(t - 1)
            if kind == 1:
                split_ht(tiles - 2)
            split_ht(tiles - 1)

        @block.tensor
        def _(pe):
            def transposes(t):
                s, v = done(t)
                pe.wait_ge(s, v)
                if t >= 2:
                    pe.wait_ge(s_mod, t - 1)
                for j in range(KT):
                    i = pe.transpose(k.bank[4 + 2 * (t % 2) + j // 4][:, (j % 4) * P:(j % 4 + 1) * P], final(t)[:, j * P:(j + 1) * P], k.ident[:, :])
                i.then_inc(s_tr, 1)

            for t in range(tiles):
                if kind == 1:
                    if t >= 2:
                        pe.wait_ge(s_dve, C * (t - 2) + 1)
                    for kt in range(KT):
                        if t == 0:
                            pe.wait_ge(s_wlow, kt + 1)
                        if kt == 0:
                            pe.wait_ge(s_low, t + 1)
                        for half in range(2):
                            n = slice(half * 512, half * 512 + 512)
                            o = k.bank[2 * (t % 2) + half][:, :]
                            pe.matmul(o, cath[:, t % 2, kt, :], wh[:, kt, n], start=kt == 0, stop=False)
                            pe.matmul(o, cath[:, t % 2, kt, :], wl[:, kt, n], start=False, stop=False)
                            i = pe.matmul(o, catl[:, t % 2, kt, :], wh[:, kt, n], start=False, stop=kt == KT - 1)
                    i.then_inc(s_yps, 1)
                if not last:
                    if kind == 1:
                        if t >= 1:
                            transposes(t - 1)
                    else:
                        transposes(t)
            if kind == 1:
                transposes(tiles - 1)


def stage_gating(nc, io, k):
    sb = Place(nc, "gate", k.after_ht)
    NU = 8
    wh, wl = sb("wh", [P, NU, KT, P], F32R), sb("wl", [P, NU, KT, P], F32R)
    RR = 4
    raw = sb("raw", [P, RR, KT, P])
    wsr, wst = sb("wsr", [P, 8, P]), sb("wst", [P, 8, P])
    bsr, bst = sb("bsr", [8, P]), sb("bst", [P, 8])
    lng, lnb = sb("lng", [P, 512]), sb("lnb", [P, 512])
    gv, bo = [sb(x, [P, 2, 512]) for x in ("gv", "bo")]
    vn, uu = [sb(x, [P, 4, 512]) for x in ("vn", "uu")]
    bot = sb("bot", [P, 2, 4, P])
    stats, mv, rstd = sb("stats", [P, 2, 6]), sb("mv", [P, 2, 2]), sb("rstd", [P, 2, 2])
    sem = lambda n: k.sem(f"gate_{n}")
    s_in, s_skew = sem("in"), sem("skew")
    s_raw = [sem(f"raw{i}") for i in range(RR)]
    s_high, s_low, s_wst, s_wsc = sem("high"), sem("low"), sem("wst"), sem("wsc")
    s_gv, s_u, s_gelu, s_gelu_u, s_dve, s_std, s_ln, s_mix, s_bo, s_bt, s_bc = [sem(x) for x in (
        "gv", "u", "gelu", "gelu_u", "dve", "std", "ln", "mix", "bo", "bt", "bc")]
    s_st = [sem("st0"), sem("st1")]
    T = XT + CT
    first = 768
    cols = [first + 512 + P * i for i in range(4)] + [first + P * i for i in range(4)]
    C = 4
    B = 3
    with nc.Block() as block:
        @block.sync
        def _(sp):
            sp.dma_start(wsr[:, :, :], io["b_ws"][0].rearrange("g p q -> p g q")).then_inc(s_in, 16)
            sp.dma_start(bsr[:, :], io["b_bs"][0]).then_inc(s_in, 16)
            sp.dma_start(lng[:, :], bass.AP(tensor=io["b_ln_g"].tensor, offset=0, ap=[[0, P], [1, 512]])).then_inc(s_in, 16)
            sp.dma_start(lnb[:, :], bass.AP(tensor=io["b_ln_b"].tensor, offset=0, ap=[[0, P], [1, 512]])).then_inc(s_in, 16)
            for u in range(NU):
                if u >= RR:
                    sp.wait_ge(s_low, u - RR + 1)
                sp.dma_start(raw[:, u % RR, :, :], io["ab_w_in"][0].rearrange("(k p) n -> p k n", p=P)[:, :, cols[u]:cols[u] + P]
                             ).then_inc(s_raw[u % RR], 16)
            for h in range(16):
                sp.dma_start(k.skew_dram[h].rearrange("c r x -> r c x"),
                             bass.AP(tensor=k.rp_dram.tensor, offset=h * RP_ROWS * RP_W + 63,
                                     ap=[[RP_W, RP_ROWS], [-1, GRID_W], [1, GRID_W]])).then_inc(s_skew, 16)
            for t in range(T):
                sp.wait_ge(s_bc, t + 1)
                sp.dma_start(k.cat_dram.rearrange("(j p) t -> p j t", p=P)[:, 4:8, t * P:(t + 1) * P], bot[:, t % 2, :, :]).then_inc(s_st[t % 2], 16)
            for i in range(2):
                sp.wait_ge(s_st[i], 16 * (T // 2))
            sp.wait_ge(s_skew, 16 * 16)

        @block.scalar
        def _(act):
            for u in range(NU):
                act.wait_ge(s_raw[u % RR], 16 * (u // RR + 1))
                act.activation(wh[:, u, :, :], raw[:, u % RR, :, :], ACT.Copy).then_inc(s_high, 1)
            for t in range(T + 2):
                if t < T:
                    act.wait_ge(s_gv, t + 1)
                    if t >= 2:
                        act.wait_ge(s_dve, C * (t - 2) + 4)
                    act.activation(gv[:, t % 2, :], k.bank[t % 2][:, :], ACT.Gelu).then_inc(s_gelu, 1)
                    act.wait_ge(s_u, t + 1)
                    if t >= 4:
                        act.wait_ge(s_bo, B * (t - 3))
                    act.activation(uu[:, t % 4, :], k.bank[2 + t % 2][:, :], ACT.Gelu).then_inc(s_gelu_u, 1)
                    act.wait_ge(s_dve, C * t + 2)
                    act.activation(rstd[:, t % 2, 0:1], mv[:, t % 2, 1:2], ACT.Sqrt, bias=k.eps[:, 0:1]).then_inc(s_std, 1)
                if t >= 2:
                    act.wait_ge(s_bt, t - 1)
                    if t >= 4:
                        act.wait_ge(s_st[t % 2], 16 * (t // 2 - 1))
                    act.activation(bot[:, t % 2, :, :], k.bank[7][:, :].rearrange("p (j q) -> p j q", q=P), ACT.Copy).then_inc(s_bc, 1)

        @block.gpsimd
        def _(pool):
            pool.wait_ge(s_in, 64)
            for t in range(T):
                v = vn[:, t % 4, :]
                pool.wait_ge(s_dve, C * t + 4)
                pool.tensor_tensor(v, v, lng[:, :], ALU.mult).then_inc(s_ln, 1)
                pool.wait_ge(s_ln, 2 * t + 1)
                pool.tensor_tensor(v, v, lnb[:, :], ALU.add).then_inc(s_ln, 1)

        @block.vector
        def _(dve):
            k.clear_last(dve)
            dve.wait_ge(s_wst, 1)
            for half in range(2):
                dve.tensor_copy(wst[:, 4 * half:4 * half + 4, :], k.bank[4 + half][:, :].rearrange("p (g q) -> p g q", q=P)).then_inc(s_wsc, 1)
            dve.tensor_copy(bst[:, :], k.bank[6][:, 0:8]).then_inc(s_wsc, 1)
            for u in range(NU):
                dve.wait_ge(s_high, u + 1)
                dve.tensor_tensor(wl[:, u, :, :], raw[:, u % RR, :, :], f32(wh[:, u, :, :]), ALU.subtract).then_inc(s_low, 1)

            def combine(t):
                dve.wait_ge(s_mix, t // 2 + 1)
                dve.wait_ge(s_wsc, 3)
                if t >= 2:
                    dve.wait_ge(s_bt, t - 1)
                for half in range(2):
                    dve.tensor_tensor(bo[:, t % 2, 256 * half:256 * (half + 1)].rearrange("p (g c) -> p g c", g=4),
                                      k.bank[4 + half][:, :].rearrange("p (g e c) -> p g e c", g=4, e=2)[:, :, t % 2, :],
                                      bst[:, 4 * half:4 * half + 4].unsqueeze(2).broadcast_to([P, 4, 64]), ALU.add).then_inc(s_bo, 1)
                dve.wait_ge(s_bo, B * t + 2)
                dve.wait_ge(s_gelu_u, t + 1)
                dve.tensor_tensor(bo[:, t % 2, :], bo[:, t % 2, :], uu[:, t % 4, :], ALU.mult).then_inc(s_bo, 1)

            for t in range(T):
                n = C * t
                dve.wait_ge(s_gelu, t + 1)
                dve.bn_stats(stats[:, t % 2, :], gv[:, t % 2, :]).then_inc(s_dve, 1)
                dve.wait_ge(s_dve, n + 1)
                dve.bn_aggr(mv[:, t % 2, :], stats[:, t % 2, :]).then_inc(s_dve, 1)
                dve.wait_ge(s_std, t + 1)
                dve.reciprocal(rstd[:, t % 2, 1:2], rstd[:, t % 2, 0:1]).then_inc(s_dve, 1)
                dve.wait_ge(s_dve, n + 3)
                if t >= 4:
                    dve.wait_ge(s_mix, t // 2 - 1)
                dve.tensor_scalar(vn[:, t % 4, :], gv[:, t % 2, :], mv[:, t % 2, 0:1], rstd[:, t % 2, 1:2],
                                  ALU.subtract, ALU.mult).then_inc(s_dve, 1)
                if t >= 2 and t % 2 == 0:
                    combine(t - 2)
                    combine(t - 1)
            combine(T - 2)
            combine(T - 1)

        @block.tensor
        def _(pe):
            pe.wait_ge(s_in, 64)
            for g in range(8):
                pe.transpose(k.bank[4 + g // 4][:, (g % 4) * P:(g % 4 + 1) * P], wsr[:, g, :], k.ident[:, :])
            pe.transpose(k.bank[6][:, 0:8], bsr[:, :], k.ident[0:8, 0:8]).then_inc(s_wst, 1)

            def mix(m):
                pe.wait_ge(s_ln, 4 * m + 4)
                pe.wait_ge(s_wsc, 3)
                if m >= 1:
                    pe.wait_ge(s_bo, B * (2 * m - 1) + 2)
                e = 2 * (m % 2)
                for g in range(8):
                    i = pe.matmul(k.bank[4 + g // 4][:, (g % 4) * P:(g % 4 + 1) * P], wst[:, g, :],
                                  vn[:, e:e + 2, g * 64:(g + 1) * 64], start=True, stop=True)
                i.then_inc(s_mix, 1)

            def turn(t):
                pe.wait_ge(s_bo, B * t + 3)
                if t >= 1:
                    pe.wait_ge(s_bc, t)
                for j in range(4):
                    i = pe.transpose(k.bank[7][:, j * P:(j + 1) * P], bo[:, t % 2, j * P:(j + 1) * P], k.ident[:, :])
                i.then_inc(s_bt, 1)

            def product(t, u0, bank, done, free):
                if t >= 2:
                    pe.wait_ge(free, t - 1)
                for kt in range(KT):
                    if t == 0 and kt == 0:
                        pe.wait_ge(s_low, u0 + 4)
                    a, b = k.hth[:, kt, t * P:(t + 1) * P], k.htl[:, kt, t * P:(t + 1) * P]
                    h, lo = wh[:, u0:u0 + 4, kt, :], wl[:, u0:u0 + 4, kt, :]
                    pe.matmul(k.bank[bank][:, :], a, h, start=kt == 0, stop=False)
                    pe.matmul(k.bank[bank][:, :], a, lo, start=False, stop=False)
                    i = pe.matmul(k.bank[bank][:, :], b, h, start=False, stop=kt == KT - 1)
                i.then_inc(done, 1)

            for t in range(T):
                product(t, 0, t % 2, s_gv, s_gelu)
                if t >= 2 and t % 2 == 0:
                    mix(t // 2 - 1)
                if t >= 3 and t % 2 == 1:
                    turn(t - 2)
                product(t, 4, 2 + t % 2, s_u, s_gelu_u)
                if t >= 2 and t % 2 == 0:
                    turn(t - 2)
            mix(T // 2 - 1)
            turn(T - 2)
            turn(T - 1)


def stage_attention(nc, io, k, layer):
    L0 = layer == 0
    tag = f"a{layer}"
    sb = Place(nc, tag, k.after_ht)
    G = 4 if L0 else 8
    wq_h, wq_l, wk_h, wk_l, wv_h, wv_l = [sb(x, [P, KT, P], F32R) for x in ("wqh", "wql", "wkh", "wkl", "wvh", "wvl")]
    wh, wl = [wv_h, wk_h, wq_h], [wv_l, wk_l, wq_l]
    raw = sb("raw", [P, 3, KT, P])
    QT = TOK if L0 else SEQ
    qh, ql = sb("qh", [P, 2, QT], F32R), sb("ql", [P, 2, QT], F32R)
    kh, kl = sb("kh", [P, TOK], F32R), sb("kl", [P, TOK], F32R)
    vt, v = sb("vt", [P, TOK]), sb("v", [P, XT + CT, P])
    ao = sb("ao", [P, QT])
    LOC = 384 if L0 else 576
    sl = sb("sl", [P, 2, LOC])
    pr = sb("pr", [P, 2, LOC + CTX])
    NKT = (LOC + P - 1) // P + CT
    ptt = sb("ptt", [P, 2, NKT, P])
    small = sb("small", [P, 2, 8])
    if L0:
        rc, rs = sb("rc", [P, SEQ]), sb("rs", [P, SEQ])
        t1, t2, rot = sb("t1", [P, 512]), sb("t2", [P, 512]), sb("rot", [P, 512])
        band = sb("band", [P, LOC])
        sink, nsink = sb("sink", [P, 8]), sb("nsink", [P, 8])
    else:
        bias = sb("bias", [P, 2, 16, GRID_W])
        mid = sb("mid", [P, 2, 9, GRID_W])
        colm, rowm = sb("colm", [P, GRID_W]), sb("rowm", [P, 9, GRID_W])
    sem = lambda n: k.sem(f"{tag}_{n}")
    s_tab = sem("tab")
    s_raw = [sem("raw_v"), sem("raw_k"), sem("raw_q")]
    s_high, s_low = [sem(f"high_{x}") for x in "vkq"], [sem(f"low_{x}") for x in "vkq"]
    s_job, s_free, s_vt, s_vtr, s_v = sem("job"), sem("free"), sem("vt"), sem("vtr"), sem("v")
    s_jh, s_rot, s_ns = sem("jh"), sem("rot"), sem("ns")
    s_bias, s_bias_in = sem("bias"), sem("bias_in")
    s_qk, s_max, s_exp, s_r, s_p, s_t, s_pta, s_ptd, s_pv, s_o, s_st, s_c = [sem(x) for x in (
        "qk", "max", "exp", "r", "p", "t", "pta", "ptd", "pv", "o", "st", "chain")]

    qgroups, kgroups = groups_of(QT), groups_of(TOK)
    NK, NQ = len(kgroups), len(qgroups)
    PER = NQ if L0 else 2 * NK + NQ
    zero_it = lambda it: isinstance(it, int) and it == 0
    has_kv = lambda it: not L0 or zero_it(it)
    EARLY = "q" if L0 else "k"

    def job_count(kind, it):
        if L0:
            return {"k": 0, "q": NK, "v": NK + NQ}[kind] if zero_it(it) else 2 * NK + NQ * it
        return it * PER + {"k": 0, "q": NK, "v": NK + NQ}[kind]
    units = []
    for hh in range(2):
        for t in range(QT // P):
            if L0:
                if t >= XT:
                    units.append((hh, t * P, 0, 0, None))
                else:
                    a, b = max(0, t - 1), min(XT, t + 2)
                    off = 0 if t else P
                    units.append((hh, t * P, a * P, (b - a) * P, band[:, off:off + (b - a) * P]))
            else:
                lo = min(max(2 * t - 4, 0), 8)
                rows = 9 if 2 <= t <= 5 else 8
                m = lo - 2 * t + 7
                tab = mid[:, hh, :, :] if rows == 9 else bias[:, hh, m:m + 8, :]
                units.append((hh, t * P, lo * GRID_W, rows * GRID_W, tab.rearrange("p r c -> p (r c)")))
    U = len(units)
    assert U % 2 == 0

    def ranges(nloc):
        if nloc == 0:
            return 0, []
        if nloc <= 384:
            return 0, [(0, 0, nloc)]
        at = 768 - nloc
        return at, [(at, 0, 512 - at), (512, 512 - at, 256)]

    w_in = io["ab_w_in"][0] if L0 else io["c_w_in"][0]
    w_view = w_in.rearrange("(k p) n -> p k n", p=P)

    def weight_dma(eng, which, it):
        dst, s = raw[:, which, :, :], s_raw[which]
        if L0:
            cols = [address(eng, it * HD + hh * 256) for hh in range(2)]
        else:
            cols = [address(eng, (2 - which) * D + it * P)]
        if not L0:
            col = cols[0]
            eng.dma_start(dst, w_view[:, :, bass.ds(col, P)]).then_inc(s, 16)
        elif which < 2:
            col = 512 + P * (1 - which)
            eng.dma_start(dst, w_view[:, :, col:col + P]).then_inc(s, 16)
        else:
            for hh in range(2):
                eng.dma_start(dst[:, :, hh * HD:(hh + 1) * HD], w_view[:, :, bass.ds(cols[hh], HD)]).then_inc(s, 16)

    TAB = 64 if L0 else 32
    RAWQ = 32 if L0 else 16
    kv_it = lambda it: 0 if L0 else it

    def over_groups(eng, body):
        body(0)
        with eng.Fori(1, G - 1) as it:
            body(it)
        body(G - 1)

    def is_last(it):
        return isinstance(it, int) and it == G - 1

    def nkt(u):
        return (units[u][3] + P - 1) // P + CT

    def bank_of(kind, j, it):
        if L0 and not zero_it(it):
            return j
        return ({"k": 0, "q": NK, "v": NK + NQ}[kind] + j) % 4

    def rotated(kind, a):
        return L0 and a < SEQ

    def rot_count(it, kind, a):
        return 3 * ((0 if kind == "k" else 2 + 2 * it) + a // 512 + 1)

    def jh_count(it, kind, j):
        if L0:
            return j if kind == "k" else NK + NQ * it + j
        return (NK + NQ) * it + (j if kind == "k" else NK + j)

    def count_free(it, kind, j):
        return jh_count(it, kind, j)

    def ptd_count(it, u):
        per = sum(nkt(x) > 4 for x in range(U))
        return it * per + sum(nkt(x) > 4 for x in range(u))

    with nc.Block() as block:
        @block.sync
        def _(sp):
            if L0:
                sp.dma_start(rc[:, :], io["rope_c"]).then_inc(s_tab, 16)
                sp.dma_start(rs[:, :], io["rope_s"]).then_inc(s_tab, 16)
                sp.dma_start(band[:, :], io["band"]).then_inc(s_tab, 16)
                sp.dma_start(sink[:, :], bass.AP(tensor=io["a_sink"].tensor, offset=0, ap=[[0, P], [1, 8]])).then_inc(s_tab, 16)
            else:
                sp.dma_start(colm[:, :], io["colm"]).then_inc(s_tab, 16)
                sp.dma_start(rowm[:, :, :].rearrange("p r c -> p (r c)"), io["rowm"]).then_inc(s_tab, 16)

            def group(it):
                if isinstance(it, int) and it == 0:
                    for which in range(3):
                        weight_dma(sp, which, 0)
                if not L0:
                    heads = [address(sp, it * 2 + hh) for hh in range(2)]
                    wait(sp, s_max, U * it)
                    for hh in range(2):
                        for rr in range(2):
                            sp.dma_start(bias[rr * 64:rr * 64 + 64, hh, :, :],
                                         k.skew_dram[bass.ds(heads[hh], 1), :, 1 - rr:17 - rr, :].rearrange("h c r x -> c (h r) x")
                                         ).then_inc(s_bias_in, 16)
                if not is_last(it):
                    slices = (2,) if L0 else (0, 1, 2)
                    for which in slices:
                        wait(sp, s_low[which], it + 1)
                    for which in slices:
                        weight_dma(sp, which, it + 1)
                rows = [address(sp, it * HD + hh * 256) for hh in range(2)] if L0 else [address(sp, it * P)]
                wait(sp, s_o, U * (it + 1))
                if L0:
                    for hh in range(2):
                        sp.dma_start(k.cat_dram[bass.ds(rows[hh], HD), 0:QT], ao[hh * HD:(hh + 1) * HD, :]).then_inc(s_st, 16)
                else:
                    sp.dma_start(k.cat_dram[bass.ds(rows[0], P), 0:QT], ao[:, :]).then_inc(s_st, 16)
            over_groups(sp, group)
            sp.wait_ge(s_st, RAWQ * G)

        @block.gpsimd
        def _(pool):
            pool.wait_ge(s_tab, TAB)

            def group(it):
                wait(pool, s_bias_in, 64 * (it + 1))
                wait(pool, s_max, U * it)
                for hh in range(2):
                    b = bias[:, hh, :, :]
                    pool.tensor_tensor(b, b, colm[:, :].unsqueeze(1).broadcast_to([P, 16, GRID_W]), ALU.add).then_inc(s_bias, 1)
                wait(pool, s_bias, 4 * it + 2)
                for hh in range(2):
                    pool.tensor_tensor(mid[:, hh, :, :], bias[:, hh, 3:12, :], rowm[:, :, :], ALU.add).then_inc(s_bias, 1)
            if not L0:
                over_groups(pool, group)

        @block.scalar
        def _(act):
            def split(which, it):
                c = it if which == 2 else kv_it(it)
                wait(act, s_raw[which], (RAWQ if which == 2 else 16) * (c + 1))
                if not zero_it(it):
                    wait(act, s_job, job_count("q", it) if L0 else it * PER)
                src, dst = raw[:, which, :, :], wh[which][:, :, :]
                if L0 and which:
                    src = src.rearrange("p k (h i e) -> p (k h) e i", h=2, e=2)
                    dst = dst.rearrange("p k (h e i) -> p (k h) e i", h=2, e=2)
                    for e in range(2):
                        i = act.activation(dst[:, :, e, :], src[:, :, e, :], ACT.Copy)
                    i.then_inc(s_high[which], 1)
                else:
                    act.activation(dst, src, ACT.Copy).then_inc(s_high[which], 1)

            def parts(it, j, kind, a, n):
                x = k.bank[bank_of(kind, j, it)][:, 0:n]
                if rotated(kind, a):
                    wait(act, s_rot, rot_count(it, kind, a))
                    x = rot[:, 0:n]
                if kind == "k":
                    act.activation(kh[:, a:a + n], x, ACT.Copy).then_inc(s_jh, 1)
                else:
                    for hh in range(2):
                        i = act.activation(qh[:, hh, a:a + n], x, ACT.Identity, scale=k.sel[:, hh:hh + 1])
                    i.then_inc(s_jh, 1)

            def heads_out(it, u):
                hh, q0, _, _, _ = units[u]
                n = it * U + u
                wait(act, s_pv, n + 1)
                if u == 0:
                    wait(act, s_st, RAWQ * it)
                rows = slice(hh * HD, (hh + 1) * HD)
                act.activation(ao[rows, q0:q0 + P], k.bank[6 + u % 2][rows, 0:P], ACT.Copy).then_inc(s_o, 1)

            def high_parts(kind, it):
                for j, (a, n) in enumerate(kgroups if kind == "k" else qgroups):
                    wait(act, s_job, job_count(kind, it) + j + 1)
                    parts(it, j, kind, a, n)

            def exps(it, u):
                hh, q0, k0, nloc, _ = units[u]
                n = it * U + u
                b = u % 2
                sm = small[:, b, :]
                wait(act, s_max, n + 1)
                wait(act, s_t, n - 1)
                p = pr[:, b, :]
                c = act.activation(p[:, nloc:nloc + CTX], k.bank[2 * b + 1][:, 256:512], ACT.Exp, bias=sm[:, 2:3],
                                   accum_out=sm[:, 4:5])
                if nloc:
                    c = act.activation(p[:, 0:nloc], sl[:, b, 0:nloc], ACT.Exp, bias=sm[:, 2:3], accum_out=sm[:, 3:4])
                if L0:
                    head = hh * 4 + it
                    c = act.activation(sm[:, 5:6], sink[:, bass.ds(head, 1)], ACT.Exp, bias=sm[:, 2:3])
                c.then_inc(s_exp, 1)

            def turned(it, u):
                n = it * U + u
                kts = nkt(u)
                m = min(4, kts)
                wait(act, s_t, n + 1)
                wait(act, s_pv, n - 1)
                act.activation(ptt[:, u % 2, 0:m, :], k.bank[4][:, 0:m * P].rearrange("p (j q) -> p j q", q=P), ACT.Copy).then_inc(s_pta, 1)

            def group(it):
                if isinstance(it, int) and it == 0:
                    for which in range(3):
                        split(which, 0)
                if zero_it(it):
                    high_parts("k", it)
                if zero_it(it) or not L0:
                    high_parts("q", it)
                if has_kv(it):
                    for j, (a, n) in enumerate(kgroups):
                        wait(act, s_job, job_count("v", it) + j + 1)
                        act.activation(vt[:, a:a + n], k.bank[bank_of("v", j, it)][:, 0:n], ACT.Copy).then_inc(s_vt, 1)
                for s in range(U + 4):
                    if 0 <= s - 4 < U:
                        heads_out(it, s - 4)
                    if 0 <= s - 2 < U:
                        turned(it, s - 2)
                    if s < U:
                        exps(it, s)
                    if s == U // 2 and not is_last(it):
                        for which in range(3):
                            if which == 2 or not L0:
                                split(which, it + 1)
                if not is_last(it):
                    high_parts(EARLY, it + 1)
            over_groups(act, group)


        @block.vector
        def _(dve):
            k.clear_last(dve)
            def split(which, it):
                c = it if which == 2 else kv_it(it)
                wait(dve, s_high[which], c + 1)
                src, dst, h = raw[:, which, :, :], wl[which][:, :, :], f32(wh[which][:, :, :])
                if L0 and which:
                    src = src.rearrange("p k (h i e) -> p (k h) e i", h=2, e=2)
                    dst = dst.rearrange("p k (h e i) -> p (k h) e i", h=2, e=2)
                    h = h.rearrange("p k (h e i) -> p (k h) e i", h=2, e=2)
                    for e in range(2):
                        i = dve.tensor_tensor(dst[:, :, e, :], src[:, :, e, :], h[:, :, e, :], ALU.subtract)
                    i.then_inc(s_low[which], 1)
                else:
                    dve.tensor_tensor(dst, src, h, ALU.subtract).then_inc(s_low[which], 1)

            def parts(it, j, kind, a, n, count):
                x = k.bank[bank_of(kind, j, it)][:, 0:n]
                if rotated(kind, a):
                    c = rot_count(it, kind, a) - 3
                    wait(dve, s_jh, count)
                    wait(dve, s_free, count_free(it, kind, j))
                    dve.tensor_tensor(t1[:, 0:n], x, rc[:, a:a + n], ALU.mult).then_inc(s_rot, 1)
                    for qd in range(4):
                        o = 32 * (qd ^ 1)
                        i = dve.tensor_tensor(t2[o:o + 32, 0:n], x[32 * qd:32 * qd + 32, :], rs[32 * qd:32 * qd + 32, a:a + n], ALU.mult)
                    i.then_inc(s_rot, 1)
                    wait(dve, s_rot, c + 2)
                    dve.tensor_tensor(rot[:, 0:n], t1[:, 0:n], t2[:, 0:n], ALU.add).then_inc(s_rot, 1)
                    wait(dve, s_rot, c + 3)
                    x = rot[:, 0:n]
                wait(dve, s_jh, count + 1)
                if kind == "k":
                    dve.tensor_tensor(kl[:, a:a + n], x, f32(kh[:, a:a + n]), ALU.subtract).then_inc(s_free, 1)
                else:
                    for hh in range(2):
                        i = dve.scalar_tensor_tensor(out=ql[:, hh, a:a + n], in0=x, scalar=k.sel[:, hh:hh + 1],
                                                     in1=f32(qh[:, hh, a:a + n]), op0=ALU.mult, op1=ALU.subtract)
                    i.then_inc(s_free, 1)

            def low_parts(kind, it):
                for j, (a, n) in enumerate(kgroups if kind == "k" else qgroups):
                    wait(dve, s_job, job_count(kind, it) + j + 1)
                    parts(it, j, kind, a, n, jh_count(it, kind, j))

            def maxima(it, u):
                hh, q0, k0, nloc, tab = units[u]
                n = it * U + u
                b = u % 2
                sm = small[:, b, :]
                wait(dve, s_qk, n + 1)
                wait(dve, s_exp, n - 1)
                wait(dve, s_p, n - 1)
                at, pieces = ranges(nloc)
                two = k.pair[b]
                c = dve.tensor_reduce(sm[:, 1:2], two[:, 768:1024], AXX, ALU.max, negate=True)
                if nloc:
                    c = dve.tensor_tensor_reduce(sl[:, b, 0:nloc], two[:, at:at + nloc], tab, 1.0, -3.0e38, ALU.add, ALU.max,
                                                 sm[:, 0:1])
                c.then_inc(s_c, 1)
                wait(dve, s_c, before_maxima(n, u) + 1)
                if L0:
                    head = hh * 4 + it
                    ns = nsink[:, bass.ds(head, 1)]
                    if nloc:
                        dve.scalar_tensor_tensor(out=sm[:, 6:7], in0=sm[:, 0:1], scalar=-1.0, in1=sm[:, 1:2], op0=ALU.mult,
                                                 op1=ALU.min).then_inc(s_c, 1)
                    else:
                        dve.tensor_copy(sm[:, 6:7], sm[:, 1:2]).then_inc(s_c, 1)
                    wait(dve, s_c, before_maxima(n, u) + 2)
                    dve.tensor_tensor(sm[:, 2:3], sm[:, 6:7], ns, ALU.min).then_inc(s_max, 1)
                else:
                    dve.scalar_tensor_tensor(out=sm[:, 2:3], in0=sm[:, 0:1], scalar=-1.0, in1=sm[:, 1:2], op0=ALU.mult,
                                             op1=ALU.min).then_inc(s_max, 1)

            hm, hs = (2, 1) if L0 else (1, 1)

            def sums(it, u):
                nloc = units[u][3]
                n = it * U + u
                sm = small[:, u % 2, :]
                wait(dve, s_exp, n + 1)
                parts_of = sm[:, 3 if nloc else 4:6 if L0 else 5]
                dve.tensor_reduce(sm[:, 6:7], parts_of, AXX, ALU.add).then_inc(s_c, 1)
                wait(dve, s_c, before_sums(n, u) + 1)
                dve.reciprocal(sm[:, 7:8], sm[:, 6:7]).then_inc(s_r, 1)
                wait(dve, s_r, n + 1)
                p = pr[:, u % 2, 0:nloc + CTX]
                dve.tensor_scalar(p, p, sm[:, 7:8], None, ALU.mult).then_inc(s_p, 1)

            def before_maxima(n, u):
                return hm * n + hs * (n - 1 if u else n)

            def before_sums(n, u):
                return hm * (n + 2 if u < U - 1 else n + 1) + hs * n

            def turned(it, u):
                n = it * U + u
                kts = nkt(u)
                if kts > 4:
                    wait(dve, s_t, n + 1)
                    wait(dve, s_pv, n - 1)
                    dve.tensor_copy(ptt[:, u % 2, 4:kts, :], k.bank[5][:, 0:(kts - 4) * P].rearrange("p (j q) -> p j q", q=P)).then_inc(s_ptd, 1)

            def group(it):
                if isinstance(it, int) and it == 0:
                    wait(dve, s_tab, TAB)
                    if L0:
                        dve.tensor_scalar(nsink[:, :], sink[:, :], -1.0, None, ALU.mult).then_inc(s_ns, 1)
                        wait(dve, s_ns, 1)
                    for which in range(3):
                        split(which, 0)
                if zero_it(it):
                    low_parts("k", it)
                if zero_it(it) or not L0:
                    low_parts("q", it)
                if has_kv(it):
                    for i, (t0, m) in enumerate(((0, 4), (4, 4), (8, 2))):
                        wait(dve, s_vtr, 3 * kv_it(it) + i + 1)
                        dve.tensor_copy(v[:, t0:t0 + m, :], k.bank[4 + i][:, 0:m * P].rearrange("p (j q) -> p j q", q=P)).then_inc(s_v, 1)
                if not L0:
                    wait(dve, s_bias, 4 * it + 4)
                for s in range(U + 3):
                    if s < U:
                        maxima(it, s)
                    if 0 <= s - 1 < U:
                        sums(it, s - 1)
                    if 0 <= s - 2 < U:
                        turned(it, s - 2)
                    if s == U // 2 and not is_last(it):
                        for which in range(3):
                            if which == 2 or not L0:
                                split(which, it + 1)
                if not is_last(it):
                    low_parts(EARLY, it + 1)
            over_groups(dve, group)


        @block.tensor
        def _(pe):
            def job(it, which, kind, j, a, n):
                b = bank_of(kind, j, it)
                first = j == 0
                if first:
                    c = it if which == 2 else kv_it(it)
                    wait(pe, s_low[which], c + 1)
                o = k.bank[b][:, 0:n]
                for kt in range(KT):
                    mv_h, mv_l = k.hth[:, kt, a:a + n], k.htl[:, kt, a:a + n]
                    pe.matmul(o, wh[which][:, kt, :], mv_h, start=kt == 0, stop=False)
                    pe.matmul(o, wh[which][:, kt, :], mv_l, start=False, stop=False)
                    i = pe.matmul(o, wl[which][:, kt, :], mv_h, start=False, stop=kt == KT - 1)
                i.then_inc(s_job, 1)

            def scores(it, u):
                hh, q0, k0, nloc, _ = units[u]
                n = it * U + u
                b = u % 2
                wait(pe, s_exp, n - 1)
                qs = slice(q0, q0 + P)
                at, pieces = ranges(nloc)
                two = k.pair[b]
                for c, kk, m in [(c, k0 + kk, m) for c, kk, m in pieces] + [(768, SEQ, CTX)]:
                    o = two[:, c:c + m]
                    pe.matmul(o, qh[:, hh, qs], kh[:, kk:kk + m], start=True, stop=False)
                    pe.matmul(o, qh[:, hh, qs], kl[:, kk:kk + m], start=False, stop=False)
                    i = pe.matmul(o, ql[:, hh, qs], kh[:, kk:kk + m], start=False, stop=True)
                i.then_inc(s_qk, 1)

            def key_tiles(u):
                hh, q0, k0, nloc, _ = units[u]
                loc = [(c, min(P, nloc - c), (k0 + c) // P) for c in range(0, nloc, P)]
                return loc + [(nloc + c * P, P, XT + c) for c in range(CT)]

            def turn(it, u):
                n = it * U + u
                wait(pe, s_p, n + 1)
                wait(pe, s_pta, n)
                wait(pe, s_ptd, ptd_count(it, u))
                for j, (c, m, _) in enumerate(key_tiles(u)):
                    i = pe.transpose(k.bank[4 + j // 4][0:m, (j % 4) * P:(j % 4 + 1) * P], pr[:, u % 2, c:c + m], k.ident[:, :])
                i.then_inc(s_t, 1)

            def values(it, u):
                hh = units[u][0]
                n = it * U + u
                wait(pe, s_pta, n + 1)
                wait(pe, s_ptd, ptd_count(it, u + 1))
                wait(pe, s_o, n - 1)
                kts = key_tiles(u)
                o = k.bank[6 + u % 2][hh * HD:(hh + 1) * HD, 0:P]
                for j, (c, m, t) in enumerate(kts):
                    i = pe.matmul(o, v[0:m, t, hh * HD:(hh + 1) * HD], ptt[0:m, u % 2, j, :], start=j == 0, stop=j == len(kts) - 1)
                i.then_inc(s_pv, 1)

            def jobs(kind, it):
                for j, (a, n) in enumerate(qgroups if kind == "q" else kgroups):
                    seq = {"k": 0, "q": NK, "v": NK + NQ}[kind] + j
                    if has_kv(it) and seq >= 4:
                        wait(pe, s_free, jh_count(it, "k", 0) + seq - 3)
                    job(it, "vkq".index(kind), kind, j, a, n)

            def early_job(it, j):
                bank = bank_of(EARLY, j, it)
                wait(pe, s_exp, U * it - 1 if bank < 2 else U * it)
                a, n = (qgroups if L0 else kgroups)[j]
                job(it, "vkq".index(EARLY), EARLY, j, a, n)

            def group(it):
                if zero_it(it):
                    jobs("k", it)
                if zero_it(it) or not L0:
                    jobs("q", it)
                if has_kv(it):
                    jobs("v", it)
                    wait(pe, s_vt, NK * (kv_it(it) + 1))
                    wait(pe, s_pta, U * it)
                    wait(pe, s_ptd, ptd_count(it, 0))
                    wait(pe, s_o, U * it)
                    for i0, (t0, m) in enumerate(((0, 4), (4, 4), (8, 2))):
                        for j in range(m):
                            i = pe.transpose(k.bank[4 + i0][:, j * P:(j + 1) * P], vt[:, (t0 + j) * P:(t0 + j + 1) * P], k.ident[:, :])
                        i.then_inc(s_vtr, 1)
                wait(pe, s_free, jh_count(it, "q", NQ - 1) + 1)
                wait(pe, s_v, 3 * (kv_it(it) + 1))
                for s in range(U + 3):
                    if s < U:
                        scores(it, s)
                    elif not is_last(it):
                        early_job(it + 1, s - U)
                    if 0 <= s - 2 < U:
                        turn(it, s - 2)
                    if 0 <= s - 3 < U:
                        values(it, s - 3)
            over_groups(pe, group)


def stage_mlp(nc, io, k, layer):
    tag = f"m{layer}"
    sb = Place(nc, tag, k.after_y)
    tiles = XT + CT if layer == 0 else XT
    groups = groups_of(tiles * P)
    NG, M = len(groups), FC // P
    J = NG * M
    NB1 = 3 if J % 3 == 0 else 4
    wah, wal = sb("wah", [P, M, KT, P], F32R), sb("wal", [P, M, KT, P], F32R)
    wbh, wbl = sb("wbh", [P, M, D], F32R), sb("wbl", [P, M, D], F32R)
    rawa, rawb = sb("rawa", [P, M, KT, P]), sb("rawb", [P, M, D])
    ath, atl = sb("ath", [P, M, tiles * P], F32R), sb("atl", [P, M, tiles * P], F32R)
    rel, sq = sb("rel", [P, 2, 512]), sb("sq", [P, 2, 512])
    stats = sb("stats", [P, 2, 2, 6])
    xin = [rawa[:, i, :, :].rearrange("p j q -> p (j q)") for i in range(2)]
    gate = rawb
    assert M >= 2
    cond = lambda t: 0 if t < XT else 1
    sem = lambda n: k.sem(f"{tag}_{n}")
    s_rawa, s_rawb = [sem(f"rawa{i}") for i in range(M)], [sem(f"rawb{i}") for i in range(M)]
    s_ahigh, s_alow, s_bhigh, s_blow = sem("ahigh"), sem("alow"), sem("bhigh"), sem("blow")
    s_h, s_relu, s_sq, s_ath, s_atl, s_w2, s_y = [sem(x) for x in ("h", "relu", "sq", "ath", "atl", "w2", "y")]
    s_gate, s_x, s_gated, s_res, s_mom = sem("gate"), [sem("x0"), sem("x1")], sem("gated"), sem("res"), sem("mom")
    w1 = io["mlp_w1"][layer].rearrange("(k p) f -> p k f", p=P)
    w2 = io["mlp_w2"][layer]
    tiles_of = lambda g: range(groups[g][0] // P, (groups[g][0] + groups[g][1]) // P)

    def over_steps(eng, body):
        body(0)
        with eng.Fori(1, NCH) as c:
            body(c)

    with nc.Block() as block:
        @block.sync
        def _(sp):
            def step(c):
                for m in range(M):
                    at = address(sp, c * FC + m * P)
                    wait(sp, s_alow, M * (c - 1) + m + 1)
                    sp.dma_start(rawa[:, m, :, :], w1[:, :, bass.ds(at, P)]).then_inc(s_rawa[m], 16)
                for m in range(M):
                    at = address(sp, c * FC + m * P)
                    wait(sp, s_blow, M * (c - 1) + m + 1)
                    sp.dma_start(rawb[:, m, :], w2[bass.ds(at, P), :]).then_inc(s_rawb[m], 16)
            over_steps(sp, step)
            sp.wait_ge(s_alow, M * NCH)
            for t in range(tiles):
                if t == 2:
                    sp.wait_ge(s_blow, M * NCH)
                    for c in range(2):
                        sp.dma_start(gate[:, c, :].rearrange("p (j q) -> p j q", q=P),
                                     bass.AP(tensor=k.gate_dram.tensor, offset=((layer * 2 + 1) * 2 * KT + c) * P,
                                             ap=[[0, P], [2 * P, KT], [1, P]])).then_inc(s_gate, 16)
                if t >= 2:
                    sp.wait_ge(s_res, t - 1)
                sp.dma_start(xin[t % 2], k.x_dram[t * P:(t + 1) * P, :]).then_inc(s_x[t % 2], 16)

        @block.scalar
        def _(act):
            def step(c):
                for m in range(M):
                    wait(act, s_rawa[m], 16 * (c + 1))
                    wait(act, s_h, J * c)
                    act.activation(wah[:, m, :, :], rawa[:, m, :, :], ACT.Copy).then_inc(s_ahigh, 1)
                for g, (a, n) in enumerate(groups):
                    if g == NG - 1:
                        for m in range(M):
                            wait(act, s_rawb[m], 16 * (c + 1))
                            wait(act, s_w2, tiles * c)
                            act.activation(wbh[:, m, :], rawb[:, m, :], ACT.Copy).then_inc(s_bhigh, 1)
                    for m in range(M):
                        j = J * c + g * M + m
                        jj = g * M + m
                        wait(act, s_h, j + 1)
                        wait(act, s_sq, j - 1)
                        wait(act, s_ath, j - 1)
                        act.activation(rel[:, m % 2, 0:n], k.bank[4 + jj % NB1][:, 0:n], ACT.Relu).then_inc(s_relu, 1)
                        wait(act, s_relu, j + 1)
                        act.activation(ath[:, m, a:a + n], rel[:, m % 2, 0:n], ACT.Square).then_inc(s_ath, 1)
            over_steps(act, step)

        @block.gpsimd
        def _(pool):
            def step(c):
                for m in range(M):
                    wait(pool, s_ahigh, M * c + m + 1)
                    pool.tensor_tensor(wal[:, m, :, :], rawa[:, m, :, :], f32(wah[:, m, :, :]), ALU.subtract).then_inc(s_alow, 1)
                for g, (a, n) in enumerate(groups):
                    for m in range(M):
                        j = J * c + g * M + m
                        wait(pool, s_relu, j + 1)
                        wait(pool, s_atl, j - 1)
                        r = rel[:, m % 2, 0:n]
                        pool.tensor_tensor(sq[:, m % 2, 0:n], r, r, ALU.mult).then_inc(s_sq, 1)
            over_steps(pool, step)
            pool.wait_ge(s_gate, 32)
            for t in range(tiles):
                pool.wait_ge(s_y, tiles * NCH + t + 1)
                pool.tensor_tensor(k.y[:, t, :], k.y[:, t, :], gate[:, cond(t), :], ALU.mult).then_inc(s_gated, 1)

        @block.vector
        def _(dve):
            k.clear_last(dve)
            def sum_tile(c, t):
                n = tiles * c + t
                wait(dve, s_w2, n + 1)
                wait(dve, s_y, n + 1)
                dve.tensor_tensor(k.y[:, t, :], k.y[:, t, :], k.pair[t % 2][:, :], ALU.add).then_inc(s_y, 1)

            def residual(t):
                y = k.y[:, t, :]
                dve.wait_ge(s_gated, t + 1)
                dve.wait_ge(s_x[t % 2], 16 * (t // 2 + 1))
                dve.scalar_tensor_tensor(out=y, in0=xin[t % 2], scalar=ALPHA, in1=y, op0=ALU.mult, op1=ALU.add).then_inc(s_res, 1)
                dve.wait_ge(s_res, t + 1)
                for half in range(2):
                    i = dve.bn_stats(stats[:, t % 2, half, :], k.y[:, t, half * 512:half * 512 + 512])
                i.then_inc(s_mom, 1)
                dve.wait_ge(s_mom, 2 * t + 1)
                dve.bn_aggr(k.mv[:, t, :], stats[:, t % 2, :, :].rearrange("p a b -> p (a b)")).then_inc(s_mom, 1)

            def step(c):
                for g, (a, n) in enumerate(groups):
                    if not (isinstance(c, int) and c == 0):
                        for t in tiles_of(g):
                            sum_tile(c - 1, t)
                    if g == NG - 1:
                        for m in range(M):
                            wait(dve, s_bhigh, M * c + m + 1)
                            dve.tensor_tensor(wbl[:, m, :], rawb[:, m, :], f32(wbh[:, m, :]), ALU.subtract).then_inc(s_blow, 1)
                    for m in range(M):
                        j = J * c + g * M + m
                        wait(dve, s_sq, j + 1)
                        wait(dve, s_ath, j + 1)
                        dve.tensor_tensor(atl[:, m, a:a + n], sq[:, m % 2, 0:n], f32(ath[:, m, a:a + n]), ALU.subtract).then_inc(s_atl, 1)
            for t in range(tiles):
                dve.memset(k.y[:, t, :], 0.0).then_inc(s_y, 1)
            over_steps(dve, step)
            for t in range(tiles + 2):
                if t < tiles:
                    sum_tile(NCH - 1, t)
                if t >= 2:
                    residual(t - 2)

        @block.tensor
        def _(pe):
            def second(c, g):
                for t in tiles_of(g):
                    n = tiles * c + t
                    wait(pe, s_y, tiles + n - 1)
                    wait(pe, s_atl, J * c + M * (g + 1))
                    wait(pe, s_blow, M * (c + 1))
                    ts = slice(t * P, t * P + P)
                    for half in range(2):
                        o, cols = k.bank[2 * (t % 2) + half][:, :], slice(half * 512, half * 512 + 512)
                        for m in range(M):
                            pe.matmul(o, ath[:, m, ts], wbh[:, m, cols], start=m == 0, stop=False)
                            pe.matmul(o, ath[:, m, ts], wbl[:, m, cols], start=False, stop=False)
                            i = pe.matmul(o, atl[:, m, ts], wbh[:, m, cols], start=False, stop=m == M - 1)
                    i.then_inc(s_w2, 1)

            def step(c):
                for g, (a, n) in enumerate(groups):
                    if not (isinstance(c, int) and c == 0):
                        second(c - 1, g)
                    for m in range(M):
                        jj = g * M + m
                        wait(pe, s_alow, M * c + m + 1)
                        wait(pe, s_relu, J * c + jj + 1 - NB1)
                        o = k.bank[4 + jj % NB1][:, 0:n]
                        for kt in range(KT):
                            xh, xl = k.hth[:, kt, a:a + n], k.htl[:, kt, a:a + n]
                            pe.matmul(o, wah[:, m, kt, :], xh, start=kt == 0, stop=False)
                            pe.matmul(o, wah[:, m, kt, :], xl, start=False, stop=False)
                            i = pe.matmul(o, wal[:, m, kt, :], xh, start=False, stop=kt == KT - 1)
                        i.then_inc(s_h, 1)
            over_steps(pe, step)
            for g in range(NG):
                second(NCH - 1, g)


def constants():
    out = {"ident": np.eye(P, dtype=np.float32)}
    tok = np.arange(SEQ)
    n_pairs = HD // 4
    freqs = (np.float32(10000.0) ** (-np.arange(n_pairs, dtype=np.float32) / n_pairs)).astype(np.float32)
    row, col = (tok // GRID_W).astype(np.float32), (tok % GRID_W).astype(np.float32)
    ang = np.concatenate([row[:, None] * freqs, col[:, None] * freqs], axis=-1).astype(np.float32)
    cos, sin = np.cos(ang).T, np.sin(ang).T
    out["rope_c"] = np.ascontiguousarray(np.tile(cos, (4, 1))).astype(np.float32)
    out["rope_s"] = np.ascontiguousarray(np.concatenate([sin, -sin, sin, -sin])).astype(np.float32)
    i, j = np.arange(P)[:, None], np.arange(P)[None, :]
    z = np.zeros((P, P))
    out["band"] = np.concatenate([np.where(j >= i, 0, NEG), z, np.where(j <= i, 0, NEG)], axis=1).astype(np.float32)
    c, c2 = np.arange(P)[:, None] % GRID_W, np.arange(GRID_W)[None, :]
    start = np.clip(c - NA_COLS // 2, 0, GRID_W - NA_COLS)
    out["colm"] = np.where((c2 >= start) & (c2 < start + NA_COLS), 0, NEG).astype(np.float32)
    rowm = np.zeros((P, 9, GRID_W), np.float32)
    rowm[0:64, 8], rowm[64:, 0] = NEG, NEG
    out["rowm"] = rowm.reshape(P, -1)
    sel = np.zeros((P, 2), np.float32)
    sel[0:64, 0] = sel[64:, 1] = HD ** -0.5
    out["sel"] = sel
    out["eps"] = np.full((P, 1), EPS, np.float32)
    return out


def build(nc, io, out):
    k = Kept(nc)
    k.out = out
    at = 16512
    small = {}
    for name, shape in (("ident", [P, P]), ("sel", [P, 2]), ("eps", [P, 1]), ("mod", [P, 2, 48, 2])):
        small[name] = nc.alloc_sbuf_tensor_at(f"kept_{name}", shape, F32, offset=at)
        at += (int(np.prod(shape[1:])) * 4 + 31) // 32 * 32
    assert at <= BASE
    k.ident, k.sel, k.eps, k.mod = (small[x] for x in ("ident", "sel", "eps", "mod"))
    k.hth = nc.alloc_sbuf_tensor_at("hth", [P, KT, TOK], F32R, offset=BASE)
    k.htl = nc.alloc_sbuf_tensor_at("htl", [P, KT, TOK], F32R, offset=BASE + KT * TOK * 4)
    k.after_ht = BASE + 2 * KT * TOK * 4
    k.y = nc.alloc_sbuf_tensor_at("y", [P, XT + CT, D], F32, offset=k.after_ht)
    k.mv = nc.alloc_sbuf_tensor_at("moments", [P, XT + CT, 2], F32, offset=k.after_ht + (XT + CT) * D * 4)
    k.after_y = k.after_ht + (XT + CT) * D * 4 + 96
    assert (XT + CT) * 2 * 4 <= 96
    pairs = [nc.alloc_psum_tensor(f"pair{i}", [P, 1024], F32) for i in range(4)]
    k.pair = pairs
    k.bank = [pairs[i // 2][:, (i % 2) * 512:(i % 2) * 512 + 512] for i in range(8)]
    k.x_dram = nc.dram_tensor("x_rows", [TOK, D], F32, kind="Internal").ap()
    k.cat_dram = nc.dram_tensor("cat_cols", [D, TOK], F32, kind="Internal").ap()
    k.gate_dram = nc.dram_tensor("gate_rows", [2, 2, 2 * KT, P], F32, kind="Internal").ap()
    k.skew_dram = nc.dram_tensor("skewed_rpb", [16, GRID_W, RP_ROWS, GRID_W], F32, kind="Internal").ap()
    k.rp_dram = nc.dram_tensor("padded_rpb", [16, RP_ROWS, RP_W], F32, kind="Internal").ap()
    stages = [(stage_modulation, ()), (stage_rows, (0, 0)), (stage_attention, (0,)), (stage_gating, ()), (stage_rows, (0, 1)),
              (stage_mlp, (0,)), (stage_rows, (0, 2)),
              (stage_attention, (1,)), (stage_rows, (1, 1)), (stage_mlp, (1,)), (stage_rows, (1, 2))]
    for stage, args in stages:
        stage(nc, io, k, *args)
        k.end_stage()


_INS = ["x", "c", "ctx", "c_ctx", "w_mod", "b_mod", "ab_w_in", "a_sink", "b_ln_g", "b_ln_b", "b_ws", "b_bs", "ab_w_out",
        "c_w_in", "c_rpb", "c_w_out", "ln1_g", "ln1_b", "mlp_w1", "mlp_w2", "ln2_g", "ln2_b"]


def kernel(**inputs):
    import concourse.bacc as bacc
    from concourse.bass_utils import run_bass_kernel_spmd

    nc = bacc.Bacc("TRN2", target_bir_lowering=False, num_devices=1)
    arrays, io = {}, {}
    for name in _INS:
        arrays[f"in_{name}"] = np.ascontiguousarray(inputs[name])
        io[name] = nc.dram_tensor(f"in_{name}", arrays[f"in_{name}"].shape, F32, kind="ExternalInput").ap()
    for name, a in constants().items():
        arrays[f"const_{name}"] = np.ascontiguousarray(a)
        io[name] = nc.dram_tensor(f"const_{name}", a.shape, F32, kind="ExternalInput").ap()
    out = nc.dram_tensor("out_x", (1, SEQ, D), F32, kind="ExternalOutput").ap()
    build(nc, io, out)
    r = run_bass_kernel_spmd(nc, [arrays], core_ids=[0])
    return r.results[0]["out_x"]
```
